# Optimizing a Trainium2 kernel written in Bass

```python
import math
import jax, jax.numpy as jnp
from jax import lax
import numpy as np

D_MODEL = 1024
BATCH = 1
SEQ = 1024
DEPTH = 1

HEAD_DIM = 64
DIFF_HEADS = 4
DIFF_VDIM = 2 * HEAD_DIM
DIFF_QK_WIDTH = DIFF_HEADS * 2 * HEAD_DIM
DIFF_WIDTH = DIFF_HEADS * DIFF_VDIM
NA_HEADS = 8
NA_WIDTH = NA_HEADS * HEAD_DIM
MIX_WIDTH = DIFF_WIDTH + NA_WIDTH
IN_COLS = 2 * DIFF_QK_WIDTH + DIFF_WIDTH + 3 * NA_WIDTH
GRID_W = 64
NA_ROWS = 8
NA_COLS = 16
MEM_TOKENS = 256
MEM_HEADS = 4
MEM_HEAD_DIM = 64
MEM_WIDTH = MEM_HEADS * MEM_HEAD_DIM
N_EXPERTS = 32
TOP_K = 4
D_FF = 1024
SWIGLU_LIMIT = 7.0
SWIGLU_ALPHA = 1.702
Q_BLOCK = 128
MOE_BLOCK = 128
RMS_EPS = 1e-5

kernel_name = "hybrid_diffattn_natten_moe_encoder"

def rmsnorm(x, g):
    xf = x.astype(jnp.float32)
    y = xf * lax.rsqrt(jnp.mean(xf * xf, axis=-1, keepdims=True) + RMS_EPS)
    return (y * g.astype(jnp.float32)).astype(x.dtype)

def alibi_slopes(n):
    return jnp.asarray(np.array([2.0 ** (-8.0 * (i + 1) / n) for i in range(n)], dtype=np.float32))

def lambda_init_for(layer):
    return 0.8 - 0.6 * math.exp(-0.3 * layer)

def diff_attention(qa, ka, va, lq1, lk1, lq2, lk2, subln_g, lam_init):
    B, S = qa.shape[:2]
    nb = S // Q_BLOCK
    scale = 1.0 / math.sqrt(HEAD_DIM)
    lam = (jnp.exp(jnp.sum(lq1.astype(jnp.float32) * lk1.astype(jnp.float32)))
           - jnp.exp(jnp.sum(lq2.astype(jnp.float32) * lk2.astype(jnp.float32))) + lam_init)
    slopes = alibi_slopes(DIFF_HEADS)
    q = qa.transpose(0, 2, 3, 1, 4)
    k = ka.transpose(0, 2, 3, 1, 4)
    v = va.transpose(0, 2, 1, 3)
    qb = q.reshape(B, DIFF_HEADS, 2, nb, Q_BLOCK, HEAD_DIM).transpose(3, 0, 1, 2, 4, 5)
    pos_k = jnp.arange(S, dtype=jnp.float32)

    def block(args):
        qblk, i = args
        pos_q = (i * Q_BLOCK + jnp.arange(Q_BLOCK)).astype(jnp.float32)
        dist = jnp.abs(pos_q[:, None] - pos_k[None, :])
        bias = -slopes[:, None, None] * dist
        s = jnp.einsum('bhcqd,bhckd->bhcqk', qblk, k).astype(jnp.float32) * scale + bias[None, :, None]
        p = jax.nn.softmax(s, axis=-1)
        a = p[:, :, 0] - lam * p[:, :, 1]
        return jnp.einsum('bhqk,bhkv->bhqv', a.astype(v.dtype), v)

    o = lax.map(block, (qb, jnp.arange(nb)))
    o = rmsnorm(o, subln_g) * (1.0 - lam_init)
    return o.transpose(1, 0, 3, 2, 4).reshape(B, S, DIFF_WIDTH)

def neighborhood_attention(qn, kn, vn, rpb):
    B, S = qn.shape[:2]
    rows = S // GRID_W
    kr = min(NA_ROWS, rows)
    scale = 1.0 / math.sqrt(HEAD_DIM)
    qg = qn.reshape(B, rows, GRID_W, NA_HEADS, HEAD_DIM).transpose(1, 0, 3, 2, 4)
    kg = kn.reshape(B, rows, GRID_W, NA_HEADS, HEAD_DIM).transpose(0, 3, 1, 2, 4)
    vg = vn.reshape(B, rows, GRID_W, NA_HEADS, HEAD_DIM).transpose(0, 3, 1, 2, 4)
    col = np.arange(GRID_W)
    col_start = np.clip(col - NA_COLS // 2, 0, GRID_W - NA_COLS)
    col_idx = col_start[:, None] + np.arange(NA_COLS)[None, :]
    dc = col_idx - col[:, None] + (NA_COLS - 1)

    def row_block(args):
        q_r, r = args
        rs = jnp.clip(r - kr // 2, 0, rows - kr)
        k_rows = lax.dynamic_slice_in_dim(kg, rs, kr, axis=2)
        v_rows = lax.dynamic_slice_in_dim(vg, rs, kr, axis=2)
        k_win = k_rows[:, :, :, col_idx]
        v_win = v_rows[:, :, :, col_idx]
        dr = rs + jnp.arange(kr) - r + (NA_ROWS - 1)
        bias = rpb[:, dr[:, None, None], dc[None]].astype(jnp.float32)
        s = jnp.einsum('bhcd,bhicjd->bhcij', q_r, k_win).astype(jnp.float32) * scale
        s = s + bias.transpose(0, 2, 1, 3)[None]
        p = jax.nn.softmax(s.reshape(B, NA_HEADS, GRID_W, kr * NA_COLS), axis=-1)
        p = p.reshape(B, NA_HEADS, GRID_W, kr, NA_COLS)
        return jnp.einsum('bhcij,bhicjd->bhcd', p.astype(v_win.dtype), v_win)

    o = lax.map(row_block, (qg, jnp.arange(rows)))
    return o.transpose(1, 0, 3, 2, 4).reshape(B, S, NA_WIDTH)

def memory_cross_attention(h, mem_n, w_mq, w_mkv, w_mo):
    B, S = h.shape[:2]
    M = mem_n.shape[1]
    q = (h @ w_mq).reshape(B, S, MEM_HEADS, MEM_HEAD_DIM)
    kv = (mem_n @ w_mkv).reshape(B, M, 2, MEM_HEADS, MEM_HEAD_DIM)
    k, v = kv[:, :, 0], kv[:, :, 1]
    s = jnp.einsum('bshd,bmhd->bhsm', q, k).astype(jnp.float32) * (1.0 / math.sqrt(MEM_HEAD_DIM))
    p = jax.nn.softmax(s, axis=-1)
    o = jnp.einsum('bhsm,bmhd->bshd', p.astype(v.dtype), v).reshape(B, S, MEM_WIDTH)
    return o @ w_mo

def moe_ffn(h, w_router, b_router, w1, b1, w2, b2):
    N, D = h.shape
    logits = (h @ w_router).astype(jnp.float32) + b_router.astype(jnp.float32)
    top_v, top_i = lax.top_k(logits, TOP_K)
    gates = jax.nn.softmax(top_v, axis=-1)
    e_flat = top_i.reshape(-1)
    g_flat = gates.reshape(-1)
    tok_flat = jnp.arange(N * TOP_K, dtype=jnp.int32) // TOP_K
    order = jnp.argsort(e_flat)
    se, st, sg = e_flat[order], tok_flat[order], g_flat[order]
    counts = jnp.zeros((N_EXPERTS,), jnp.int32).at[e_flat].add(1)
    pcounts = ((counts + MOE_BLOCK - 1) // MOE_BLOCK) * MOE_BLOCK
    starts = jnp.cumsum(counts) - counts
    pends = jnp.cumsum(pcounts)
    pstarts = pends - pcounts
    dest = pstarts[se] + (jnp.arange(N * TOP_K, dtype=jnp.int32) - starts[se])
    P = N * TOP_K + N_EXPERTS * MOE_BLOCK
    nblk = P // MOE_BLOCK
    row_tok = jnp.full((P,), N, jnp.int32).at[dest].set(st)
    h_pad = jnp.concatenate([h, jnp.zeros((1, D), h.dtype)], axis=0)
    xin = h_pad[row_tok].reshape(nblk, MOE_BLOCK, D)
    blk_start = jnp.arange(nblk, dtype=jnp.int32) * MOE_BLOCK
    blk_e = jnp.minimum(jnp.sum(blk_start[:, None] >= pends[None, :], axis=1), N_EXPERTS - 1)

    def expert_block(args):
        xb, e = args
        gu = xb @ w1[e] + b1[e]
        gate = jnp.minimum(gu[:, :D_FF], SWIGLU_LIMIT)
        lin = jnp.clip(gu[:, D_FF:], -SWIGLU_LIMIT, SWIGLU_LIMIT)
        act = gate * jax.nn.sigmoid(SWIGLU_ALPHA * gate) * (lin + 1.0)
        return act @ w2[e] + b2[e]

    y_pad = lax.map(expert_block, (xin, blk_e)).reshape(P, D)
    y = y_pad[dest] * sg[:, None].astype(y_pad.dtype)
    return jax.ops.segment_sum(y, st, num_segments=N)

def setup_inputs(seed: int = 0) -> dict:
    key = jax.random.key(seed)
    ks = jax.random.split(key, 24)
    L = DEPTH
    nrm = lambda k, shape, s: jax.random.normal(k, shape, jnp.float32) * s
    gain = lambda k, shape: 1.0 + nrm(k, shape, 0.05)
    return {
        "x": nrm(ks[0], (BATCH, SEQ, D_MODEL), 1.0),
        "mem": nrm(ks[1], (BATCH, MEM_TOKENS, D_MODEL), 1.0),
        "norm_mix_g": gain(ks[2], (L, D_MODEL)),
        "w_in": nrm(ks[3], (L, D_MODEL, IN_COLS), D_MODEL ** -0.5),
        "lambda_q1": nrm(ks[4], (L, HEAD_DIM), 0.1),
        "lambda_k1": nrm(ks[5], (L, HEAD_DIM), 0.1),
        "lambda_q2": nrm(ks[6], (L, HEAD_DIM), 0.1),
        "lambda_k2": nrm(ks[7], (L, HEAD_DIM), 0.1),
        "subln_g": gain(ks[8], (L, DIFF_VDIM)),
        "rpb": nrm(ks[9], (L, NA_HEADS, 2 * NA_ROWS - 1, 2 * NA_COLS - 1), 0.1),
        "w_out": nrm(ks[10], (L, MIX_WIDTH, D_MODEL), MIX_WIDTH ** -0.5),
        "norm_mem_q_g": gain(ks[11], (L, D_MODEL)),
        "norm_mem_kv_g": gain(ks[12], (L, D_MODEL)),
        "w_mq": nrm(ks[13], (L, D_MODEL, MEM_WIDTH), D_MODEL ** -0.5),
        "w_mkv": nrm(ks[14], (L, D_MODEL, 2 * MEM_WIDTH), D_MODEL ** -0.5),
        "w_mo": nrm(ks[15], (L, MEM_WIDTH, D_MODEL), MEM_WIDTH ** -0.5),
        "norm_ffn_g": gain(ks[16], (L, D_MODEL)),
        "w_router": nrm(ks[17], (L, D_MODEL, N_EXPERTS), D_MODEL ** -0.5),
        "b_router": nrm(ks[18], (L, N_EXPERTS), 0.01),
        "w1": nrm(ks[19], (L, N_EXPERTS, D_MODEL, 2 * D_FF), D_MODEL ** -0.5),
        "b1": nrm(ks[20], (L, N_EXPERTS, 2 * D_FF), 0.01),
        "w2": nrm(ks[21], (L, N_EXPERTS, D_FF, D_MODEL), D_FF ** -0.5),
        "b2": nrm(ks[22], (L, N_EXPERTS, D_MODEL), 0.01),
        "norm_final_g": gain(ks[23], (D_MODEL,)),
    }

def reference(x, mem, norm_mix_g, w_in, lambda_q1, lambda_k1, lambda_q2, lambda_k2, subln_g, rpb,
              w_out, norm_mem_q_g, norm_mem_kv_g, w_mq, w_mkv, w_mo, norm_ffn_g, w_router, b_router,
              w1, b1, w2, b2, norm_final_g):
    B, S = x.shape[:2]
    splits = np.cumsum([DIFF_QK_WIDTH, DIFF_QK_WIDTH, DIFF_WIDTH, NA_WIDTH, NA_WIDTH])
    for l in range(DEPTH):
        h = rmsnorm(x, norm_mix_g[l])
        qkv = h @ w_in[l]
        qa, ka, va, qn, kn, vn = jnp.split(qkv, splits, axis=-1)
        qa = qa.reshape(B, S, DIFF_HEADS, 2, HEAD_DIM)
        ka = ka.reshape(B, S, DIFF_HEADS, 2, HEAD_DIM)
        va = va.reshape(B, S, DIFF_HEADS, DIFF_VDIM)
        qn = qn.reshape(B, S, NA_HEADS, HEAD_DIM)
        kn = kn.reshape(B, S, NA_HEADS, HEAD_DIM)
        vn = vn.reshape(B, S, NA_HEADS, HEAD_DIM)
        o_diff = diff_attention(qa, ka, va, lambda_q1[l], lambda_k1[l], lambda_q2[l], lambda_k2[l],
                                subln_g[l], lambda_init_for(l))
        o_na = neighborhood_attention(qn, kn, vn, rpb[l])
        x = x + jnp.concatenate([o_diff, o_na], axis=-1) @ w_out[l]
        hm = rmsnorm(x, norm_mem_q_g[l])
        mem_n = rmsnorm(mem, norm_mem_kv_g[l])
        x = x + memory_cross_attention(hm, mem_n, w_mq[l], w_mkv[l], w_mo[l])
        hf = rmsnorm(x, norm_ffn_g[l]).reshape(B * S, D_MODEL)
        x = x + moe_ffn(hf, w_router[l], b_router[l], w1[l], b1[l], w2[l], b2[l]).reshape(B, S, D_MODEL)
    return rmsnorm(x, norm_final_g)


_drawn_inputs = setup_inputs


def setup_inputs(seed=0):
    import zlib

    import numpy as np

    out = dict(_drawn_inputs(seed))
    spreads = {}
    factors = {'norm_mem_q_g': 2.988,
     'norm_mem_kv_g': 2.774,
     'b1': 23.273,
     'b2': 26.735,
     'b_router': 3.725}
    for name, (base, spread) in spreads.items():
        noise = np.random.default_rng([zlib.crc32(name.encode()), seed]).standard_normal(out[name].shape)
        drawn = base * np.exp(spread * noise) if base else spread * noise
        out[name] = __import__('jax').numpy.asarray(drawn.astype(out[name].dtype))
    for name, factor in factors.items():
        out[name] = (out[name] * factor).astype(out[name].dtype)
    return out
```

```python
import math
from contextlib import ExitStack

import concourse.bass as bass
from concourse import mybir

F32 = mybir.dt.float32
U32 = mybir.dt.uint32
I32 = mybir.dt.int32
ALU = mybir.AluOpType
ACT = mybir.ActivationFunctionType
AX = mybir.AxisListType

P = 128
D = 1024
S = 1024
KD = D // P
NT = S // P
HALF = 512
HD = 64
DIFF_HEADS = 4
NA_PAIRS = 4
GRID_W = 64
NA_ROWS, NA_COLS = 8, 16
RPB_R, RPB_C = 2 * NA_ROWS - 1, 2 * NA_COLS - 1
RPB_HEAD = RPB_R * RPB_C
RPB_PAD = 64
RPB_LEN = 3840 + 2 * RPB_PAD
MEM = 256
MH = 4
E = 32
TOPK = 4
FF = 1024
KF = FF // P
EPS = 1e-5
LIMIT = 7.0
ALPHA = 1.702
LAM_INIT = 0.8 - 0.6 * math.exp(-0.3 * 0)
QSCALE = 1.0 / math.sqrt(HD)
NEG = -1.0e30
LOWEST = -3.0e38

CAP = 192
CAP2 = CAP - P
OVER = 128
N_OVER = -(-(S - CAP) // OVER)
POSN = CAP + N_OVER * OVER
EC = E + 2
NOBODY = 1 << 20
VARIANTS = (96, 128, 160, 192)

PRIMED = 1

G_MIX, G_MEMQ, G_MEMKV, G_FFN, G_SUB = 0, 8, 16, 24, 32


class Link:

    def __init__(self, eng, sem):
        self.eng, self.sem, self.base, self.n, self.it, self.per = eng, sem, 0, 0, None, 0

    def __call__(self, ins):
        self.n += 1
        ins.then_inc(self.sem, 1)
        at = self.base + self.n
        self.eng.wait_ge(self.sem, at if self.it is None else self.it * self.per + at)

    def enter(self, it, per):
        self.base += self.n
        self.n, self.it, self.per = 0, it, per

    def leave(self, trips):
        assert self.n == self.per, (self.n, self.per)
        self.base += trips * self.per
        self.n, self.it = 0, None


def stage_sems(sem, stage, names):
    return {n: sem(f"{stage}_{n}") for n in names.split()}


def na_window(t):
    r = 2 * t
    lo = min(max(r - NA_ROWS // 2, 0), S // GRID_W - NA_ROWS)
    hi = min(max(r + 1 - NA_ROWS // 2, 0), S // GRID_W - NA_ROWS)
    if lo == hi:
        return lo * GRID_W, NA_ROWS * GRID_W, (lo - r + NA_ROWS - 1 - 1) * GRID_W
    return lo * GRID_W, (NA_ROWS + 1) * GRID_W, NA_EDGE


NA_EDGE = 14 * GRID_W
NA_TABLE = NA_EDGE + (NA_ROWS + 1) * GRID_W


def encoder_layer(nc, x, mem, norm_mix_g, w_in, lambda_q1, lambda_k1, lambda_q2, lambda_k2, subln_g, rpb,
                  w_out, norm_mem_q_g, norm_mem_kv_g, w_mq, w_mkv, w_mo, norm_ffn_g, w_router, b_router,
                  w1, b1, w2, b2, norm_final_g, col_mask, out):
    ctx = ExitStack()
    with ctx:
        def sb(name, shape, dt=F32):
            return ctx.enter_context(nc.sbuf_tensor(name, shape, dt))

        def sem(name):
            return ctx.enter_context(nc.semaphore(name))

        rpb_pad = nc.dram_tensor("rpb_pad", [RPB_LEN], F32, kind="Internal").ap()
        na_bias = nc.dram_tensor("na_bias", [2 * NA_PAIRS, P, NA_TABLE], F32, kind="Internal").ap()
        h_rows = nc.dram_tensor("h_rows", [S, D], F32, kind="Internal").ap()
        slot_choice = nc.dram_tensor("slot_choice", [POSN * EC, 1], U32, kind="Internal").ap()
        y_rows = nc.dram_tensor("y_rows", [S * TOPK, D], F32, kind="Internal").ap()

        xres = sb("xres", [P, NT, D])
        hT = sb("hT", [P, KD, S])
        arena = sb("arena", [P, 3 * 8192])
        work_len = 9088 + 256
        work = sb("work", [P, work_len])
        ident = sb("ident", [P, P])
        vecT = sb("vecT", [P, P])
        mixg = sb("mixg", [P, KD])
        b1T = sb("b1T", [P, 4 * P])
        b2T = sb("b2T", [P, 2 * P])
        kmz = sb("kmz", [P, 2, 2, MEM])
        vmem = sb("vmem", [P, 2, MEM])
        st = sb("st", [P, 96])
        PS = ctx.enter_context(nc.psum_tensor("PS", [P, 8, HALF], F32))

        def bank(b, n=1):
            return PS[:, b:b + n, :].rearrange("p a b -> p (a b)")

        def carver(region, total):
            at = [0]

            def carve(size, pattern=None, **kw):
                a = region[:, at[0]:at[0] + size]
                at[0] += size
                assert at[0] <= total, (at[0], total)
                return a.rearrange(pattern, **kw) if pattern else a
            return carve

        r0, r1, r2 = (arena[:, i * 8192:(i + 1) * 8192] for i in range(3))
        wA = r0.rearrange("p (k g n) -> p k g n", k=KD, g=2)
        wB = r1.rearrange("p (k g n) -> p k g n", k=KD, g=2)
        wD = r2.rearrange("p (k n) -> p k n", k=KF)
        c = carver(r0, 8192)
        wmkv = c(4096, "p (k n) -> p k n", k=KD)
        memT = c(2048, "p (k n) -> p k n", k=KD)
        mrows = c(2048, "p (a n) -> p a n", a=2)
        wout = r0.rearrange("p (k n) -> p k n", k=KD)
        c = carver(r2, 8192)
        vrows = c(P)
        brows = c(6 * P, "p (a n) -> p a n", a=6)
        lamv = c(4 * HD, "p (a n) -> p a n", a=4)
        mix = r2.rearrange("p (t n) -> p t n", t=NT)
        c = carver(r1, 8192)
        wqkv = c(3 * KD * P, "p (j k n) -> p j k n", j=3, k=KD)
        qT = c(S)
        xn = c(3 * D, "p (a n) -> p a n", a=3)
        pT2 = xn[:, 0:2, :]
        acomb = xn[:, 2, :]
        v_sb = c(S, "p (t n) -> p t n", t=NT)
        c = carver(work, work_len)
        kz = c(2 * S, "p (a n) -> p a n", a=2)
        sp = c(4 * D, "p (a n) -> p a n", a=4)
        tables = c(2 * NA_TABLE)
        na_tab = tables.rearrange("p (a n) -> p a n", a=2)
        alibi = tables[:, 0:1920]
        junk = c(P)
        sub_ms = c(DIFF_HEADS * NT)
        sub_rs = c(DIFF_HEADS * NT)
        cmask = c(GRID_W)
        c = carver(r1, 8192)
        wmq = c(2048, "p (k n) -> p k n", k=KD)
        wmo = c(2048, "p (k n) -> p k n", k=2)
        c = carver(work, work_len)
        qmT = c(2 * S, "p (a n) -> p a n", a=2)
        mp = c(2 * D, "p (a n) -> p a n", a=2)
        mpT = c(D)
        om = c(MEM)
        omT = c(MEM)
        xn2 = c(3 * D, "p (a n) -> p a n", a=3)
        wrt = c(KD * E, "p (k n) -> p k n", k=KD)
        c = carver(work, work_len)
        logit = c(NT * E, "p (t e) -> p t e", t=NT)
        oneh = c(TOPK * NT * E, "p (k n) -> p k n", k=TOPK)
        msum = c(NT * E)
        slotm = c(NT * E)
        prod = c(2 * NT * E, "p (k n) -> p k n", k=2)
        ones = c(P)
        before = c(P)
        iota_e = c(E)
        top8 = c(NT * 8, "p (t k) -> p t k", t=NT)
        top8i = c(NT * 8).bitcast(U32).rearrange("p (t k) -> p t k", t=NT)
        slot_f = c(TOPK * NT, "p (k t) -> p k t", k=TOPK)
        c = carver(work, work_len)
        xg = c(2 * D, "p (a n) -> p a n", a=2)
        actT = c(KF * CAP, "p (k n) -> p k n", k=KF)
        yT = c(KD * CAP, "p (k n) -> p k n", k=KD)
        c = carver(hT[:, :, :].rearrange("p k n -> p (k n)"), 8192)
        xT = c(KD * CAP, "p (k n) -> p k n", k=KD)
        ysb = c(2 * D, "p (a n) -> p a n", a=2)
        ep = c(8 * CAP, "p (b j n) -> p b j n", b=2, j=4)
        idx_now = c(4).bitcast(U32)
        choice_all = c((2 + N_OVER) * EC).bitcast(U32)
        token_all = c((2 + N_OVER) * EC).bitcast(U32)

        def place_tables(table):
            return (table[:, 0:EC], table[0:CAP2, EC:2 * EC],
                    table[:, 2 * EC:].rearrange("p (j c) -> p j c", j=N_OVER))

        choice_a, choice_b, choice_o = place_tables(choice_all)
        token_a, token_b, token_o = place_tables(token_all)
        gfin = r0[:, 0:D]
        yg = r1.rearrange("p (a n) -> p a n", a=8)
        facc = r2.rearrange("p (a n) -> p a n", a=8)
        cnt = sb("cnt", [P, E + 1], I32)
        gates = sb("gates", [P, NT, TOPK])
        slot_u = sb("slot_u", [P, TOPK, NT], U32)
        choice = sb("choice", [P, NT, TOPK], U32)
        brt = sb("brt", [P, E])

        ssq, rms, rstd = st[:, 0:10], st[:, 10:20], st[:, 20:30]
        nmax, rsum, rinv = st[:, 30:34], st[:, 34:38], st[:, 38:42]
        lam = st[:, 44:50]
        coef = st[:, 42:44]
        rmax = st[:, 74:78]
        ssq8 = st[:, 50:58]
        cross_max = st[:, 70:74]

        x_in = [sem(f"x_in{t}") for t in range(NT)]
        setup = stage_sems(sem, "setup", "vec_cleared vec_in lam_in mem_in wmkv_in rpb_zero rpb_in bias_made small_in "
                 "vecT_made vecT_copied mkv_made mkv_copied alibi_made lam_dots lam_exp ident_made pads_zero kz_zero")
        norms = [stage_sems(sem, f"norm{i}", "meansq root rinv scaled turned copied") for i in range(3)]
        na = stage_sems(sem, "na", "w_in tab_in proj proj_copied scores biased exp turned turned_copied out out_copied")
        diff = stage_sems(sem, "diff", "w_in proj proj_copied scores biased exp comb turned turned_copied out out_copied squared meansq")
        mixed = stage_sems(sem, "mix", "wout_in root scaled turned copied made added")
        cross = stage_sems(sem, "cross", "wmq_in wmo_in q q_copied scores max exp turned turned_copied out out_copied "
                  "out_turned out_turned_copied made added")
        route = stage_sems(sem, "route", "w_in logits masked placed slots gate_in gate_exp table_clear scattered "
                  "idx_in tokens_made cnt_made gates_made consts")
        moe = stage_sems(sem, "moe", "rows_free picked wA_in wB_in wD_in gathered x_turned x_copied up gated sig act down y_copied "
                  "y_turned y_moved named stored")
        over = stage_sems(sem, "over", "picked wA_in wB_in wD_in gathered x_turned x_copied up gated sig act down y_copied "
                  "y_turned y_moved named stored idle")
        final = stage_sems(sem, "final", "g_in sum squares root scaled stored cleared")
        final["rows_in"] = [sem(f"final_rows_in{a}") for a in range(2)]
        h_stored = [sem(f"h_stored{a}") for a in range(3)]
        dve_link, pool_link = sem("dve_link"), sem("pool_link")
        wait_passed = sem("wait_passed")

        def carried(eng):
            eng.sem_inc(wait_passed, 1)

        block = ctx.enter_context(nc.Block())

        @block.sync
        def _(sp_):
            for t in range(NT):
                sp_.dma_start(xres[:, t, :], x[0, t * P:(t + 1) * P, :]).then_inc(x_in[t], 16)
            sp_.wait_ge(setup["vec_cleared"], 1)
            for row, g in ((G_MIX, norm_mix_g), (G_MEMQ, norm_mem_q_g), (G_MEMKV, norm_mem_kv_g), (G_FFN, norm_ffn_g)):
                sp_.dma_start(vrows[row:row + KD, :], g[0, :].rearrange("(c p) -> c p", p=P)).then_inc(setup["vec_in"], 16)
            sp_.dma_start(vrows[G_SUB:G_SUB + 1, :], subln_g[0:1, :]).then_inc(setup["vec_in"], 16)
            sp_.dma_start(brows[:, 0:4, :], b1[0].rearrange("e (f p) -> (e f) p", p=P)
                          .rearrange("(c r) p -> r c p", r=P)).then_inc(setup["vec_in"], 16)
            sp_.dma_start(brows[:, 4:6, :], b2[0].rearrange("e (f p) -> (e f) p", p=P)
                          .rearrange("(c r) p -> r c p", r=P)).then_inc(setup["vec_in"], 16)
            sp_.dma_start(mrows[:, :, :], mem[0].rearrange("(a p) n -> p a n", p=P)).then_inc(setup["mem_in"], 16)
            sp_.dma_start(wmkv[:, :, :], w_mkv[0].rearrange("(k p) n -> p k n", p=P)).then_inc(setup["wmkv_in"], 16)
            sp_.wait_ge(setup["rpb_zero"], 16)
            sp_.dma_start(rpb_pad[RPB_PAD:RPB_PAD + 8 * RPB_HEAD], rpb[0].rearrange("h r c -> (h r c)")).then_inc(setup["rpb_in"], 16)

            def load_head(base, i, s, j0=0):
                for j, first in enumerate(base):
                    sp_.dma_start(wqkv[:, j, :, :], w_in[0, :, bass.ds(first + i * P, P)]
                                  .rearrange("(k p) n -> p k n", p=P)).then_inc(s, 16)

            def spread_bias(q):
                for half in range(2):
                    for first, n, low in ((0, 14, 1), (NA_EDGE, NA_ROWS + 1, 3)):
                        start = RPB_PAD + (low - half) * RPB_C + NA_COLS - 1
                        src = rpb_pad[bass.ds(start - q, 2 * NA_PAIRS * RPB_HEAD)].rearrange("(h n) -> h n", h=2 * NA_PAIRS)[
                            :, 0:n * RPB_C].rearrange("h (r c) -> h r c", c=RPB_C)
                        src = bass.AP(tensor=src.tensor, offset=src.offset, ap=[[RPB_HEAD, 2 * NA_PAIRS], [RPB_C, n], [1, GRID_W]])
                        sp_.dma_start(na_bias[:, bass.ds(q + half * HD, 1), first:first + n * GRID_W]
                                      .rearrange("h a (r c) -> h (a r) c", r=n), src).then_inc(setup["bias_made"], 16)

            QS = GRID_W // DIFF_HEADS
            sp_.wait_ge(setup["rpb_in"], 16)
            load_head((0, 512, 1024), 0, diff["w_in"])
            with sp_.Fori(0, QS) as q:
                spread_bias(q)
            with sp_.Fori(1, DIFF_HEADS) as i:
                sp_.wait_ge(diff["proj"], i * 6)
                load_head((0, 512, 1024), i, diff["w_in"])
                with sp_.Fori(0, QS) as q:
                    spread_bias(i * QS + q)

            def load_table(i):
                sp_.dma_start(na_tab, na_bias[bass.ds(i * 2, 2), :, :].rearrange("a p n -> p a n")).then_inc(na["tab_in"], 16)

            sp_.wait_ge(diff["proj"], 6 * DIFF_HEADS)
            load_head((1536, 2048, 2560), 0, na["w_in"])
            sp_.wait_ge(setup["bias_made"], 16 * 4 * GRID_W)
            sp_.wait_ge(diff["biased"], 16 * DIFF_HEADS)
            load_table(0)
            with sp_.Fori(1, NA_PAIRS) as i:
                sp_.wait_ge(na["proj"], i * 6)
                load_head((1536, 2048, 2560), i, na["w_in"])
                sp_.wait_ge(na["biased"], i * 16)
                load_table(i)
            sp_.wait_ge(setup["mkv_made"], 3)
            sp_.dma_start(wout[:, :, :], w_out[0].rearrange("(k p) n -> p k n", p=P)).then_inc(mixed["wout_in"], 16)
            sp_.wait_ge(na["out"], 16 * NA_PAIRS)
            sp_.dma_start(wmq[:, :, :], w_mq[0].rearrange("(k p) n -> p k n", p=P)).then_inc(cross["wmq_in"], 16)
            sp_.dma_start(wmo[:, :, :], w_mo[0].rearrange("(k p) n -> p k n", p=P)).then_inc(cross["wmo_in"], 16)
            sp_.dma_start(wrt[:, :, :], w_router[0].rearrange("(k p) n -> p k n", p=P)).then_inc(route["w_in"], 16)

            def load_up(buf, first, e, s):
                for g in range(2):
                    sp_.dma_start(buf[:, :, g, :], w1[0, bass.ds(e, 1), :, g * FF + first:g * FF + first + HALF]
                                  .rearrange("a (k p) n -> p (a k) n", p=P)).then_inc(s, 16)

            def load_down(e, s):
                sp_.dma_start(wD[:, :, :], w2[0, bass.ds(e, 1), :, :].rearrange("a (k p) n -> p (a k) n", p=P)).then_inc(s, 16)

            sp_.wait_ge(mixed["turned"], NT)
            load_down(0, moe["wD_in"])
            sp_.wait_ge(mixed["made"], NT)
            load_up(wA, 0, 0, moe["wA_in"])
            sp_.wait_ge(cross["made"], NT)
            load_up(wB, HALF, 0, moe["wB_in"])
            for t in range(NT):
                sp_.wait_ge(norms[2]["scaled"], t + 1)
                sp_.dma_start(h_rows[t * P:(t + 1) * P, :], xn2[:, t % 3, :]).then_inc(h_stored[t % 3], 16)
            sp_.wait_ge(route["scattered"], 16 * TOPK * NT)
            sp_.dma_start(choice_a[:, :], slot_choice[0:P * EC, :].rearrange("(p c) o -> p (c o)", c=EC)).then_inc(route["idx_in"], 16)
            sp_.dma_start(choice_b[:, :], slot_choice[P * EC:CAP * EC, :].rearrange("(p c) o -> p (c o)", c=EC)).then_inc(route["idx_in"], 16)
            sp_.dma_start(choice_o[:, :, :], slot_choice[CAP * EC:POSN * EC, :].rearrange("(j p c) o -> p j (c o)", c=EC, p=OVER)).then_inc(route["idx_in"], 16)
            with sp_.Fori(0, E - 1) as e:
                sp_.wait_ge(moe["up"], e * 8 + 4)
                load_up(wA, 0, e + 1, moe["wA_in"])
                sp_.wait_ge(moe["up"], e * 8 + 8)
                load_up(wB, HALF, e + 1, moe["wB_in"])
                sp_.wait_ge(moe["down"], e * 8 + 8)
                load_down(e + 1, moe["wD_in"])
            sp_.wait_ge(moe["down"], 8 * E)
            most = sp_.value_load(cnt[0:1, E:E + 1], min_val=0, max_val=S)
            with sp_.If(most > CAP):
                with sp_.Fori(0, E) as e:
                    n = sp_.value_load(cnt[0:1, bass.ds(e, 1)], min_val=0, max_val=S)
                    for j in range(N_OVER):
                        with sp_.If(n > CAP + j * OVER):
                            sp_.wait_ge(over["idle"], e * N_OVER + j + PRIMED)
                            load_up(wA, 0, e, over["wA_in"])
                            load_up(wB, HALF, e, over["wB_in"])
                            load_down(e, over["wD_in"])
                            item = e * N_OVER + j
                            for s, v in ((over["wA_in"], 32), (over["wB_in"], 32), (over["wD_in"], 16)):
                                sp_.wait_ge(s, item * v + v)
                            carried(sp_)
                        with sp_.Else():
                            sp_.sem_inc(over["wA_in"], 32)
                            sp_.sem_inc(over["wB_in"], 32)
                            sp_.sem_inc(over["wD_in"], 16)
                        sp_.nop()
                sp_.wait_ge(over["idle"], E * N_OVER + PRIMED)
            with sp_.Else():
                sp_.nop()
            sp_.dma_start(gfin, norm_final_g.rearrange("(a n) -> a n", a=1).to_broadcast([P, D])).then_inc(final["g_in"], 16)
            sp_.wait_ge(moe["stored"], 32 * (E + 1))
            for t in range(NT):
                if t >= 2:
                    sp_.wait_ge(final["sum"], t - 1)
                sp_.dma_start(yg[:, (t % 2) * TOPK:(t % 2 + 1) * TOPK, :], y_rows[t * P * TOPK:(t + 1) * P * TOPK, :]
                              .rearrange("(p k) n -> p k n", k=TOPK)).then_inc(final["rows_in"][t % 2], 16)
            for t in range(NT):
                sp_.wait_ge(final["scaled"], t + 1)
                sp_.dma_start(out[0, t * P:(t + 1) * P, :], facc[:, t, :]).then_inc(final["stored"], 16)
            sp_.wait_ge(final["stored"], 16 * NT)

        @block.gpsimd
        def _(pool):
            link = Link(pool, pool_link)
            pool.memset(vrows, 0.0).then_inc(setup["vec_cleared"], 1)
            pool.wait_ge(setup["vec_cleared"], 1)
            link(pool.memset(sp[:, 0, :], 0.0))
            pool.dma_start(rpb_pad.rearrange("(p n) -> p n", p=P), sp[:, 0, 0:RPB_LEN // P]).then_inc(setup["rpb_zero"], 16)
            pool.dma_start(lamv[:, 0, :], lambda_q1[0:1, :].to_broadcast([P, HD])).then_inc(setup["lam_in"], 16)
            pool.dma_start(lamv[:, 1, :], lambda_k1[0:1, :].to_broadcast([P, HD])).then_inc(setup["lam_in"], 16)
            pool.dma_start(lamv[:, 2, :], lambda_q2[0:1, :].to_broadcast([P, HD])).then_inc(setup["lam_in"], 16)
            pool.dma_start(lamv[:, 3, :], lambda_k2[0:1, :].to_broadcast([P, HD])).then_inc(setup["lam_in"], 16)
            pool.dma_start(brt[:, :], b_router[0:1, :].to_broadcast([P, E])).then_inc(setup["small_in"], 16)
            pool.dma_start(cmask, col_mask).then_inc(setup["small_in"], 16)
            link(pool.memset(ident[:, :], 0.0))
            pool.affine_select(out=ident[:, :], in_=ident[:, :], compare_op=ALU.not_equal, fill=1.0, base=0,
                               pattern=[[-1, P]], channel_multiplier=1).then_inc(setup["ident_made"], 1)
            pool.wait_ge(setup["ident_made"], 1)
            link(pool.iota(choice[:, :, :], pattern=[[TOPK * P, NT], [1, TOPK]], base=0, channel_multiplier=TOPK))
            link(pool.memset(kz[0:HD, 1, :], 0.0))
            link(pool.memset(kz[HD:P, 0, :], 0.0))
            link(pool.memset(kmz[0:HD, 1, :, :], 0.0))
            pool.memset(kmz[HD:P, 0, :, :], 0.0).then_inc(setup["kz_zero"], 1)
            pool.wait_ge(setup["kz_zero"], 1)
            empty = sp[:, 1, 0:POSN * EC // P].bitcast(U32)
            link(pool.memset(empty, NOBODY))
            pool.dma_start(slot_choice.rearrange("(p c) o -> p (c o)", p=P), empty).then_inc(route["table_clear"], 16)
            pool.wait_ge(route["table_clear"], 16)
            pool.wait_ge(setup["rpb_zero"], 16)
            pool.iota(alibi, pattern=[[-1, 1920]], base=896, channel_multiplier=1,
                      allow_small_or_imprecise_dtypes=True).then_inc(setup["alibi_made"], 1)
            pool.wait_ge(setup["alibi_made"], 1)
            pool.wait_ge(diff["comb"], NT * DIFF_HEADS)
            pool.memset(sp[:, :, 576:640], 0.0).then_inc(setup["pads_zero"], 1)
            pool.wait_ge(setup["pads_zero"], 1)
            pool.wait_ge(cross["added"], 2 * NT)
            link(pool.memset(ones, 1.0))
            pool.affine_select(out=before, in_=ones, compare_op=ALU.is_gt, fill=0.0, base=0, pattern=[[1, P]],
                               channel_multiplier=-1).then_inc(route["consts"], 1)
            pool.wait_ge(route["consts"], 1)
            pool.iota(iota_e, pattern=[[1, E]], base=0, channel_multiplier=0,
                      allow_small_or_imprecise_dtypes=True).then_inc(route["consts"], 1)
            pool.wait_ge(route["table_clear"], 16)
            pool.wait_ge(route["slots"], 1)
            for k in range(TOPK):
                for t in range(NT):
                    pool.indirect_dma_start(out=slot_choice, out_offset=bass.IndirectOffsetOnAxis(slot_u[:, k, t:t + 1], 0),
                                            in_=choice[:, t, k:k + 1], in_offset=None).then_inc(route["scattered"], 16)
            for t3 in range(3):
                pool.wait_ge(h_stored[t3], 16 * len(range(t3, NT, 3)))
            pool.wait_ge(route["gates_made"], 1)
            pool.memset(xg[:, :, :], 0.0).then_inc(final["cleared"], 1)
            pool.wait_ge(final["cleared"], 1)
            pool.memset(yT[:, :, :], 0.0).then_inc(final["cleared"], 1)
            pool.wait_ge(final["cleared"], 2)

            def store(a, b, ns, n):
                pool.tensor_copy(idx_now[:, 2:3], a).then_inc(ns["named"], 1)
                if b is not None:
                    pool.wait_ge(ns["named"], 2 * n + 1)
                    pool.tensor_copy(idx_now[0:CAP2, 3:4], b).then_inc(ns["named"], 1)
                pool.wait_ge(ns["named"], n + 1 if b is None else 2 * n + 2)
                pool.wait_ge(ns["y_moved"], (2 * n + 2 if b is None else 4 * n + 4) + PRIMED)
                carried(pool)
                pool.indirect_dma_start(out=y_rows, out_offset=bass.IndirectOffsetOnAxis(idx_now[:, 2:3], 0), in_=ysb[:, 0, :],
                                        in_offset=None, bounds_check=S * TOPK - 1, oob_is_err=False).then_inc(ns["stored"], 16)
                if b is not None:
                    pool.indirect_dma_start(out=y_rows, out_offset=bass.IndirectOffsetOnAxis(idx_now[0:CAP2, 3:4], 0),
                                            in_=ysb[0:CAP2, 1, :], in_offset=None, bounds_check=S * TOPK - 1,
                                            oob_is_err=False).then_inc(ns["stored"], 16)

            def gather(a, b, ns, n):
                pool.tensor_copy(idx_now[:, 0:1], a).then_inc(ns["picked"], 1)
                if b is not None:
                    pool.wait_ge(ns["picked"], 2 * n + 1)
                    pool.tensor_copy(idx_now[0:CAP2, 1:2], b).then_inc(ns["picked"], 1)
                pool.wait_ge(ns["picked"], n + 1 if b is None else 2 * n + 2)
                carried(pool)
                pool.indirect_dma_start(out=xg[:, 0, :], out_offset=None, in_=h_rows,
                                        in_offset=bass.IndirectOffsetOnAxis(idx_now[:, 0:1], 0), bounds_check=S - 1,
                                        oob_is_err=False).then_inc(ns["gathered"], 16)
                if b is not None:
                    pool.indirect_dma_start(out=xg[0:CAP2, 1, :], out_offset=None, in_=h_rows,
                                            in_offset=bass.IndirectOffsetOnAxis(idx_now[0:CAP2, 1:2], 0), bounds_check=S - 1,
                                            oob_is_err=False).then_inc(ns["gathered"], 16)

            pool.sem_inc(moe["rows_free"], PRIMED)
            pool.sem_inc(over["idle"], PRIMED)
            pool.wait_ge(route["tokens_made"], 1)
            gather(token_a[:, 1:2], token_b[:, 1:2], moe, 0)
            with pool.Fori(0, E) as e:
                pool.wait_ge(moe["x_turned"], e * 4 + 4)
                gather(token_a[:, bass.ds(e + 2, 1)], token_b[:, bass.ds(e + 2, 1)], moe, e + 1)
                store(choice_a[:, bass.ds(e, 1)], choice_b[:, bass.ds(e, 1)], moe, e)
                pool.wait_ge(moe["stored"], e * 32 + 32)
                pool.sem_inc(moe["rows_free"], 1)
            store(choice_a[:, E:E + 1], choice_b[:, E:E + 1], moe, E)
            pool.wait_ge(moe["x_turned"], 4 * (E + 1))
            pool.wait_ge(moe["stored"], 32 * (E + 1))
            most = pool.value_load(cnt[0:1, E:E + 1], min_val=0, max_val=S)
            with pool.If(most > CAP):
                with pool.Fori(0, E) as e:
                    n = pool.value_load(cnt[0:1, bass.ds(e, 1)], min_val=0, max_val=S)
                    for j in range(N_OVER):
                        with pool.If(n > CAP + j * OVER):
                            gather(token_o[:, j, bass.ds(e + 1, 1)], None, over, e * N_OVER + j)
                            store(choice_o[:, j, bass.ds(e + 1, 1)], None, over, e * N_OVER + j)
                            pool.wait_ge(over["stored"], (e * N_OVER + j) * 16 + 16)
                            pool.sem_inc(over["idle"], 1)
                        with pool.Else():
                            for s, v in ((over["picked"], 1), (over["gathered"], 16), (over["named"], 1), (over["stored"], 16)):
                                pool.sem_inc(s, v)
                            pool.sem_inc(over["idle"], 1)
                        pool.nop()
            with pool.Else():
                pool.nop()

        @block.tensor
        def _(pe):
            def norm_turn(ns, buf, n_tiles, first_wait=None):
                for t in range(n_tiles):
                    pe.wait_ge(ns["scaled"], t + 1)
                    if t >= 2:
                        pe.wait_ge(ns["copied"], t - 1)
                    b = 2 * (t % 2)
                    for k in range(KD):
                        last = pe.transpose(bank(b, 2)[:, k * P:(k + 1) * P], buf[:, t % 3, k * P:(k + 1) * P], ident[:, :])
                    last.then_inc(ns["turned"], 1)

            pe.wait_ge(setup["ident_made"], 1)
            pe.wait_ge(setup["vec_in"], 7 * 16)
            pe.transpose(bank(4)[:, 0:P], vrows, ident[:, :])
            for a in range(4):
                pe.transpose(bank(5)[:, a * P:(a + 1) * P], brows[:, a, :], ident[:, :])
            for a in range(2):
                last = pe.transpose(bank(6)[:, a * P:(a + 1) * P], brows[:, 4 + a, :], ident[:, :])
            last.then_inc(setup["vecT_made"], 1)
            norm_turn(norms[0], xn, NT + 2)
            pe.wait_ge(norms[0]["copied"], NT + 2)
            pe.wait_ge(setup["wmkv_in"], 16)
            pe.wait_ge(setup["vecT_copied"], 3)
            for c2 in range(2):
                for k in range(KD):
                    last = pe.matmul(bank(4 + c2)[:, 0:MEM], wmkv[:, k, c2 * P:(c2 + 1) * P], memT[:, k, :],
                                     start=(k == 0), stop=(k == KD - 1))
                last.then_inc(setup["mkv_made"], 1)
            for a in range(2):
                for k in range(KD):
                    last = pe.matmul(bank(6)[:, a * MEM:(a + 1) * MEM], memT[:, k, a * P:(a + 1) * P],
                                     wmkv[:, k, MEM:2 * MEM], start=(k == 0), stop=(k == KD - 1))
            last.then_inc(setup["mkv_made"], 1)
            pe.wait_ge(setup["mkv_copied"], 4)

            def project(i, ns):
                pe.wait_ge(ns["w_in"], i * 48 + 48)
                for j in range(2):
                    for n in range(2):
                        for k in range(KD):
                            last = pe.matmul(bank(2 * j + n), wqkv[:, j, k, :], hT[:, k, n * HALF:(n + 1) * HALF],
                                             start=(k == 0), stop=(k == KD - 1))
                        last.then_inc(ns["proj"], 1)
                for n in range(2):
                    for t in range(4):
                        for k in range(KD):
                            last = pe.matmul(bank(4 + n)[:, t * P:(t + 1) * P], hT[:, k, (4 * n + t) * P:(4 * n + t + 1) * P],
                                             wqkv[:, 2, k, :], start=(k == 0), stop=(k == KD - 1))
                    last.then_inc(ns["proj"], 1)
                pe.wait_ge(ns["proj_copied"], i * 8 + 8)

            with pe.Fori(0, DIFF_HEADS) as i:
                project(i, diff)

                def scores(t):
                    for c2 in range(2):
                        if t >= 1:
                            pe.wait_ge(diff["biased"], i * 16 + 2 * (t - 1) + c2 + 1)
                        for n in range(2):
                            last = pe.matmul(bank(2 * c2 + n), qT[:, t * P:(t + 1) * P], kz[:, c2, n * HALF:(n + 1) * HALF],
                                             start=True, stop=True)
                        last.then_inc(diff["scores"], 1)

                def turn(t):
                    pe.wait_ge(diff["comb"], i * 8 + t + 1)
                    if t >= 1:
                        pe.wait_ge(diff["turned_copied"], i * 8 + t)
                    for a in range(NT):
                        last = pe.transpose(bank(4, 2)[:, a * P:(a + 1) * P], acomb[:, a * P:(a + 1) * P], ident[:, :])
                    last.then_inc(diff["turned"], 1)

                def weigh(t):
                    pe.wait_ge(diff["turned_copied"], i * 8 + t + 1)
                    if t >= 2:
                        pe.wait_ge(diff["out_copied"], i * 8 + t - 1)
                        pe.wait_ge(diff["squared"], i * 8 + t - 1)
                    for a in range(NT):
                        last = pe.matmul(bank(6 + t % 2)[:, 0:P], pT2[:, t % 2, a * P:(a + 1) * P], v_sb[:, a, :],
                                         start=(a == 0), stop=(a == NT - 1))
                    last.then_inc(diff["out"], 1)

                scores(0)
                for t in range(NT):
                    if t + 1 < NT:
                        scores(t + 1)
                    if t >= 1:
                        weigh(t - 1)
                    turn(t)
                weigh(NT - 1)
                pe.wait_ge(diff["out_copied"], i * 8 + 8)
                pe.wait_ge(diff["squared"], i * 8 + 8)

            with pe.Fori(0, NA_PAIRS) as i:
                project(i, na)

                def scores(u):
                    t, c2 = divmod(u, 2)
                    first, width, _ = na_window(t)
                    b = 2 * (u % 2)
                    if u >= 2:
                        pe.wait_ge(na["biased"], i * 16 + u - 1)
                    for a in range(0, width, HALF):
                        w = min(HALF, width - a)
                        last = pe.matmul(bank(b, 2)[:, a:a + w], qT[:, t * P:(t + 1) * P],
                                         kz[:, c2, first + a:first + a + w], start=True, stop=True)
                    last.then_inc(na["scores"], 1)

                def turn(u):
                    chunks = -(-na_window(u // 2)[1] // P)
                    pe.wait_ge(na["exp"], i * 16 + u + 1)
                    if u >= 1:
                        pe.wait_ge(na["turned_copied"], i * 16 + u)
                    for a in range(chunks):
                        last = pe.transpose(bank(4, 2)[:, a * P:(a + 1) * P], sp[:, u % 4, a * P:(a + 1) * P], ident[:, :])
                    last.then_inc(na["turned"], 1)

                def weigh(u):
                    t, c2 = divmod(u, 2)
                    first, width, _ = na_window(t)
                    chunks = -(-width // P)
                    pe.wait_ge(na["turned_copied"], i * 16 + u + 1)
                    if u >= 2:
                        pe.wait_ge(na["out_copied"], i * 16 + u - 1)
                    for a in range(chunks):
                        last = pe.matmul(bank(6 + u % 2)[:, 0:HD], pT2[:, u % 2, a * P:(a + 1) * P],
                                         v_sb[:, first // P + a, c2 * HD:(c2 + 1) * HD], start=(a == 0), stop=(a == chunks - 1))
                    last.then_inc(na["out"], 1)

                scores(0)
                scores(1)
                for u in range(16):
                    turn(u)
                    if u + 2 < 16:
                        scores(u + 2)
                    if u >= 1:
                        weigh(u - 1)
                weigh(15)
                pe.wait_ge(na["out_copied"], i * 16 + 16)

            for t in range(NT):
                pe.wait_ge(mixed["scaled"], t + 1)
                if t >= 2:
                    pe.wait_ge(mixed["copied"], t - 1)
                for k in range(KD):
                    last = pe.transpose(bank(2 * (t % 2), 2)[:, k * P:(k + 1) * P], mix[:, t, k * P:(k + 1) * P], ident[:, :])
                last.then_inc(mixed["turned"], 1)
            pe.wait_ge(mixed["wout_in"], 16)
            for t in range(NT):
                pe.wait_ge(mixed["copied"], t + 1)
                if t >= 2:
                    pe.wait_ge(mixed["added"], t - 1)
                for n in range(2):
                    for k in range(KD):
                        last = pe.matmul(bank(4 + 2 * (t % 2) + n), hT[:, k, t * P:(t + 1) * P],
                                         wout[:, k, n * HALF:(n + 1) * HALF], start=(k == 0), stop=(k == KD - 1))
                last.then_inc(mixed["made"], 1)
            norm_turn(norms[1], xn2, NT)

            pe.wait_ge(cross["wmq_in"], 16)
            pe.wait_ge(norms[1]["copied"], NT)
            for j in range(4):
                c2, n = divmod(j, 2)
                for k in range(KD):
                    last = pe.matmul(bank(j), wmq[:, k, c2 * P:(c2 + 1) * P], hT[:, k, n * HALF:(n + 1) * HALF],
                                     start=(k == 0), stop=(k == KD - 1))
                last.then_inc(cross["q"], 1)
            pe.wait_ge(cross["q_copied"], 4)
            pe.wait_ge(cross["wmo_in"], 16)

            def cross_scores(t):
                if t >= 2:
                    pe.wait_ge(cross["exp"], t - 1)
                for hd in range(MH):
                    last = pe.matmul(bank(2 * (t % 2), 2)[:, hd * MEM:(hd + 1) * MEM], qmT[:, hd // 2, t * P:(t + 1) * P],
                                     kmz[:, hd % 2, hd // 2, :], start=True, stop=True)
                last.then_inc(cross["scores"], 1)

            def cross_made(t):
                pe.wait_ge(cross["out_turned_copied"], t + 1)
                for n in range(2):
                    for k in range(2):
                        last = pe.matmul(bank(4 + n), omT[:, k * P:(k + 1) * P], wmo[:, k, n * HALF:(n + 1) * HALF],
                                         start=(k == 0), stop=(k == 1))
                last.then_inc(cross["made"], 1)

            cross_scores(0)
            for t in range(NT):
                if t + 1 < NT:
                    cross_scores(t + 1)
                pe.wait_ge(cross["exp"], t + 1)
                if t >= 1:
                    pe.wait_ge(cross["added"], 2 * t)
                for a in range(8):
                    last = pe.transpose(bank(4, 2)[:, a * P:(a + 1) * P], mp[:, t % 2, a * P:(a + 1) * P], ident[:, :])
                last.then_inc(cross["turned"], 1)
                pe.wait_ge(cross["turned_copied"], t + 1)
                for hd in range(MH):
                    for a in range(2):
                        last = pe.matmul(bank(6)[:, hd * HD:(hd + 1) * HD], mpT[:, (2 * hd + a) * P:(2 * hd + a + 1) * P],
                                         vmem[:, a, hd * HD:(hd + 1) * HD], start=(a == 0), stop=(a == 1))
                last.then_inc(cross["out"], 1)
                pe.wait_ge(cross["out_copied"], t + 1)
                for a in range(2):
                    last = pe.transpose(bank(7)[:, a * P:(a + 1) * P], om[:, a * P:(a + 1) * P], ident[:, :])
                last.then_inc(cross["out_turned"], 1)
                cross_made(t)

            norm_turn(norms[2], xn2, NT)
            pe.wait_ge(route["w_in"], 16)
            for t in range(NT):
                pe.wait_ge(norms[2]["copied"], t + 1)
                for k in range(KD):
                    last = pe.matmul(bank(4)[:, t * E:(t + 1) * E], hT[:, k, t * P:(t + 1) * P], wrt[:, k, :],
                                     start=(k == 0), stop=(k == KD - 1))
            last.then_inc(route["logits"], 1)
            pe.wait_ge(route["masked"], 1)
            pe.wait_ge(route["consts"], 2)
            pe.matmul(bank(5)[:, 0:NT * E], before, msum, start=True, stop=False, skip_group_check=True)
            for t in range(NT - 1):
                for t2 in range(t + 1, NT):
                    pe.matmul(bank(5)[:, t2 * E:(t2 + 1) * E], ones, msum[:, t * E:(t + 1) * E], start=False,
                              stop=(t == NT - 2), skip_group_check=True)
            for t in range(NT):
                last = pe.matmul(bank(6)[:, 0:E], ones, msum[:, t * E:(t + 1) * E], start=(t == 0), stop=(t == NT - 1))
            last.then_inc(route["placed"], 1)
            pe.wait_ge(route["cnt_made"], 1)
            for b in range(4):
                pe.matmul(bank(b), ident[:, :], hT[:, 0, 0:HALF], start=True, stop=True)

            def x_turn(ns, n, with_b=True):
                pe.wait_ge(ns["gathered"], n * (32 if with_b else 16) + (32 if with_b else 16))
                for q in range(4):
                    if q == 0:
                        pe.wait_ge(ns["x_copied"], n * 4 + PRIMED)
                    if q >= 2:
                        pe.wait_ge(ns["x_copied"], n * 4 + q - 1 + PRIMED)
                    b = bank(4 + q % 2)
                    for kk in range(2):
                        k = 2 * q + kk
                        last = pe.transpose(b[:, kk * CAP:kk * CAP + P], xg[:, 0, k * P:(k + 1) * P], ident[:, :])
                        if with_b:
                            last = pe.transpose(b[:, kk * CAP + P:(kk + 1) * CAP], xg[0:CAP2, 1, k * P:(k + 1) * P],
                                                ident[0:CAP2, 0:CAP2])
                    last.then_inc(ns["x_turned"], 1)

            def y_turn(ns, n, copied, with_b=True):
                steps = 4 if with_b else 2
                pe.wait_ge(ns["y_copied"], copied + PRIMED)
                for q in range(steps):
                    a, half = divmod(q, 2)
                    if q == 0:
                        pe.wait_ge(ns["y_moved"], n * steps + PRIMED)
                    if q >= 2:
                        pe.wait_ge(ns["y_moved"], n * steps + q - 1 + PRIMED)
                        carried(pe)
                    rows = P if a == 0 else CAP2
                    for kk in range(4):
                        k = 4 * half + kk
                        last = pe.transpose(bank(6 + half)[0:rows, kk * P:(kk + 1) * P], yT[:, k, a * P:a * P + rows], ident[:, :])
                    last.then_inc(ns["y_turned"], 1)

            def up(ns, n, cols):
                for m in range(KF):
                    buf = wA if m < 4 else wB
                    if m == 0:
                        pe.wait_ge(ns["wA_in"], n * 32 + 32)
                    if m == 4:
                        pe.wait_ge(ns["wB_in"], n * 32 + 32)
                    if m >= 2:
                        pe.wait_ge(ns["gated"], n * 8 + m - 1)
                    for g in range(2):
                        for k in range(KD):
                            last = pe.matmul(bank(m % 2)[:, g * CAP:g * CAP + cols], buf[:, k, g, (m % 4) * P:(m % 4 + 1) * P],
                                             xT[:, k, 0:cols], start=(k == 0), stop=(k == KD - 1))
                    last.then_inc(ns["up"], 1)

            def down(ns, n, cols):
                pe.wait_ge(ns["wD_in"], n * 16 + 16)
                pe.wait_ge(ns["act"], n * 8 + 8)
                for m in range(KD):
                    if m >= 2:
                        pe.wait_ge(ns["y_copied"], n * 8 + m - 1 + PRIMED)
                    for k in range(KF):
                        last = pe.matmul(bank(2 + m % 2)[:, 0:cols], wD[:, k, m * P:(m + 1) * P], actT[:, k, 0:cols],
                                         start=(k == 0), stop=(k == KF - 1))
                    last.then_inc(ns["down"], 1)

            def by_count(n, step, some=VARIANTS):
                if len(some) == 1:
                    step(some[0])
                    return
                with pe.If(n <= some[0]):
                    step(some[0])
                with pe.Else():
                    by_count(n, step, some[1:])
                    pe.nop()

            pe.wait_ge(final["cleared"], 2)
            x_turn(moe, 0)
            with pe.Fori(0, E) as e:
                n = pe.value_load(cnt[0:1, bass.ds(e, 1)], min_val=0, max_val=S)
                pe.wait_ge(moe["x_copied"], e * 4 + 4 + PRIMED)
                by_count(n, lambda cols: up(moe, e, cols))
                x_turn(moe, e + 1)
                y_turn(moe, e, e * 8)
                by_count(n, lambda cols: down(moe, e, cols))
            y_turn(moe, E, E * 8)
            most = pe.value_load(cnt[0:1, E:E + 1], min_val=0, max_val=S)
            with pe.If(most > CAP):
                pe.wait_ge(moe["x_copied"], 4 * (E + 1) + PRIMED)
                pe.wait_ge(moe["y_moved"], 4 * (E + 1) + PRIMED)
                with pe.Fori(0, E) as e:
                    n = pe.value_load(cnt[0:1, bass.ds(e, 1)], min_val=0, max_val=S)
                    for j in range(N_OVER):
                        item = e * N_OVER + j
                        with pe.If(n > CAP + j * OVER):
                            x_turn(over, item, with_b=False)
                            pe.wait_ge(over["x_copied"], item * 4 + 4 + PRIMED)
                            up(over, item, OVER)
                            down(over, item, OVER)
                            y_turn(over, item, item * 8 + 8, with_b=False)
                            pe.wait_ge(over["y_moved"], item * 2 + 2 + PRIMED)
                        with pe.Else():
                            for s, v in ((over["x_turned"], 4), (over["up"], 8), (over["down"], 8), (over["y_turned"], 2)):
                                pe.sem_inc(s, v)
                        pe.nop()
            with pe.Else():
                pe.nop()

        @block.scalar
        def _(act):
            def norm_act(ns, src, buf, n_tiles):
                for t in range(n_tiles):
                    act.wait_ge(ns["meansq"], t + 1)
                    act.activation(rms[:, t:t + 1], rms[:, t:t + 1], ACT.Sqrt).then_inc(ns["root"], 1)
                    act.wait_ge(ns["rinv"], t + 1)
                    act.activation(buf[:, t % 3, :], src(t), ACT.Copy, scale=rstd[:, t:t + 1]).then_inc(ns["scaled"], 1)

            norm_act(norms[0], lambda t: xres[:, t, :] if t < NT else mrows[:, t - NT, :], xn, NT + 2)
            act.wait_ge(setup["kz_zero"], 1)
            act.wait_ge(setup["mkv_made"], 3)
            for c2 in range(2):
                for h in range(2):
                    rows = slice(h * HD, (h + 1) * HD)
                    act.activation(kmz[rows, h, c2, :], bank(4 + c2)[rows, 0:MEM], ACT.Copy).then_inc(setup["mkv_copied"], 1)
            act.activation(vmem[:, :, :].rearrange("p a n -> p (a n)"), bank(6), ACT.Copy).then_inc(setup["mkv_copied"], 1)
            act.wait_ge(setup["lam_dots"], 2)
            act.activation(lam[:, 2:4], lam[:, 0:2], ACT.Exp).then_inc(setup["lam_exp"], 1)

            def project_copy(i, ns):
                for n in range(2):
                    act.wait_ge(ns["proj"], i * 6 + 1 + n)
                    act.activation(qT[:, n * HALF:(n + 1) * HALF], bank(n), ACT.Copy, scale=QSCALE).then_inc(ns["proj_copied"], 1)
                for n in range(2):
                    act.wait_ge(ns["proj"], i * 6 + 3 + n)
                    for h in range(2):
                        rows = slice(h * HD, (h + 1) * HD)
                        act.activation(kz[rows, h, n * HALF:(n + 1) * HALF], bank(2 + n)[rows, :], ACT.Copy).then_inc(ns["proj_copied"], 1)
                for n in range(2):
                    act.wait_ge(ns["proj"], i * 6 + 5 + n)
                    act.activation(v_sb[:, 4 * n:4 * n + 4, :].rearrange("p t n -> p (t n)"), bank(4 + n), ACT.Copy).then_inc(ns["proj_copied"], 1)

            with act.Fori(0, DIFF_HEADS) as i:
                project_copy(i, diff)

                def copy_turned(t):
                    act.wait_ge(diff["turned"], i * 8 + t + 1)
                    if t >= 2:
                        act.wait_ge(diff["out"], i * 8 + t - 1)
                    act.activation(pT2[:, t % 2, :], bank(4, 2), ACT.Copy).then_inc(diff["turned_copied"], 1)

                def square(t):
                    act.wait_ge(diff["out_copied"], i * 8 + t + 1)
                    if t >= 1:
                        act.wait_ge(diff["squared"], i * 8 + t)
                    act.activation(junk, bank(6 + t % 2)[:, 0:P], ACT.Square, scale=rinv[:, 2 * (t % 2):2 * (t % 2) + 1],
                                   accum_out=ssq8[:, t:t + 1]).then_inc(diff["squared"], 1)

                for t in range(NT):
                    for c2 in range(2):
                        a = 2 * (t % 2) + c2
                        act.wait_ge(diff["biased"], i * 16 + 2 * t + c2 + 1)
                        act.activation(sp[:, a, :], sp[:, a, :], ACT.Exp, bias=nmax[:, a:a + 1],
                                       accum_out=rsum[:, a:a + 1]).then_inc(diff["exp"], 1)
                    if t >= 1:
                        copy_turned(t - 1)
                    if t >= 2:
                        square(t - 2)
                copy_turned(NT - 1)
                square(NT - 2)
                square(NT - 1)
                act.wait_ge(diff["squared"], i * 8 + 8)
                carried(act)

            with act.Fori(0, NA_PAIRS) as i:
                project_copy(i, na)

                def copy_turned(u):
                    if u >= 2:
                        act.wait_ge(na["out"], i * 16 + u - 1)
                    act.wait_ge(na["turned"], i * 16 + u + 1)
                    w = -(-na_window(u // 2)[1] // P) * P
                    act.activation(pT2[:, u % 2, 0:w], bank(4, 2)[:, 0:w], ACT.Copy).then_inc(na["turned_copied"], 1)

                for u in range(16):
                    width = na_window(u // 2)[1]
                    act.wait_ge(na["biased"], i * 16 + u + 1)
                    act.activation(sp[:, u % 4, 0:width], sp[:, u % 4, 0:width], ACT.Exp, bias=nmax[:, u % 4:u % 4 + 1],
                                   accum_out=rsum[:, u % 4:u % 4 + 1]).then_inc(na["exp"], 1)
                    if u >= 1:
                        copy_turned(u - 1)
                copy_turned(15)

            act.wait_ge(diff["meansq"], DIFF_HEADS)
            act.activation(sub_ms, sub_ms, ACT.Sqrt).then_inc(mixed["root"], 1)
            norm_act(norms[1], lambda t: xres[:, t, :], xn2, NT)

            for j in range(4):
                c2, n = divmod(j, 2)
                act.wait_ge(cross["q"], j + 1)
                act.activation(qmT[:, c2, n * HALF:(n + 1) * HALF], bank(j), ACT.Copy, scale=QSCALE).then_inc(cross["q_copied"], 1)
            for t in range(NT):
                act.wait_ge(cross["max"], t + 1)
                if t >= 2:
                    act.wait_ge(cross["turned"], t - 1)
                for hd in range(MH):
                    last = act.activation(mp[:, t % 2, hd * MEM:(hd + 1) * MEM], bank(2 * (t % 2), 2)[:, hd * MEM:(hd + 1) * MEM],
                                          ACT.Exp, bias=nmax[:, hd:hd + 1], accum_out=rsum[:, hd:hd + 1])
                last.then_inc(cross["exp"], 1)
                act.wait_ge(cross["turned"], t + 1)
                act.activation(mpT, bank(4, 2), ACT.Copy).then_inc(cross["turned_copied"], 1)
                act.wait_ge(cross["out_turned"], t + 1)
                act.activation(omT, bank(7)[:, 0:MEM], ACT.Copy).then_inc(cross["out_turned_copied"], 1)

            def norm_act_stored():
                for t in range(NT):
                    act.wait_ge(norms[2]["meansq"], t + 1)
                    act.activation(rms[:, t:t + 1], rms[:, t:t + 1], ACT.Sqrt).then_inc(norms[2]["root"], 1)
                    act.wait_ge(norms[2]["rinv"], t + 1)
                    act.activation(xn2[:, t % 3, :], xres[:, t, :], ACT.Copy, scale=rstd[:, t:t + 1]).then_inc(norms[2]["scaled"], 1)

            norm_act_stored()
            act.wait_ge(route["gate_in"], 1)
            act.activation(gates[:, :, :], gates[:, :, :], ACT.Exp).then_inc(route["gate_exp"], 1)

            def sigmoids(ns, n):
                for m in range(KF):
                    act.wait_ge(ns["gated"], n * 8 + m + 1)
                    if m >= 2:
                        act.wait_ge(ns["act"], n * 8 + m - 1)
                    act.activation(ep[:, m % 2, 2, :], ep[:, m % 2, 0, :], ACT.Sigmoid, scale=ALPHA).then_inc(ns["sig"], 1)

            def y_move(ns, n, with_b=True):
                steps = 4 if with_b else 2
                if with_b:
                    act.wait_ge(ns["rows_free"], n + PRIMED)
                for q in range(steps):
                    a, half = divmod(q, 2)
                    rows = P if a == 0 else CAP2
                    act.wait_ge(ns["y_turned"], n * steps + q + 1)
                    act.activation(ysb[0:rows, a, half * HALF:(half + 1) * HALF], bank(6 + half)[0:rows, :], ACT.Copy).then_inc(ns["y_moved"], 1)

            def bias_copy(ns, n, e):
                for m in range(KD):
                    act.wait_ge(ns["down"], n * 8 + m + 1)
                    act.activation(yT[:, m, :], bank(2 + m % 2)[:, 0:CAP], ACT.Identity,
                                   bias=b2T[:, bass.ds(e * 8 + m, 1)]).then_inc(ns["y_copied"], 1)

            for stage in (moe, over):
                act.sem_inc(stage["y_copied"], PRIMED)
                act.sem_inc(stage["y_moved"], PRIMED)
            act.wait_ge(final["cleared"], 2)
            with act.Fori(0, E) as e:
                sigmoids(moe, e)
                y_move(moe, e)
                bias_copy(moe, e, e)
            y_move(moe, E)
            most = act.value_load(cnt[0:1, E:E + 1], min_val=0, max_val=S)
            with act.If(most > CAP):
                with act.Fori(0, E) as e:
                    n = act.value_load(cnt[0:1, bass.ds(e, 1)], min_val=0, max_val=S)
                    for j in range(N_OVER):
                        item = e * N_OVER + j
                        with act.If(n > CAP + j * OVER):
                            sigmoids(over, item)
                            bias_copy(over, item, e)
                            y_move(over, item, with_b=False)
                        with act.Else():
                            for s, v in ((over["sig"], 8), (over["y_copied"], 8), (over["y_moved"], 2)):
                                act.sem_inc(s, v)
                        act.nop()
            with act.Else():
                act.nop()
            for t in range(NT):
                act.wait_ge(final["squares"], t + 1)
                act.activation(rms[:, t:t + 1], rms[:, t:t + 1], ACT.Sqrt).then_inc(final["root"], 1)

        def vector_program(dve):
            link = Link(dve, dve_link)

            def norm_dve(ns, src, buf, n_tiles, dest, gain, ready):
                def mean_square(t):
                    ready(t)
                    if t >= 3:
                        dve.wait_ge(ns["turned"], t - 2)
                        if ns is norms[2]:
                            dve.wait_ge(h_stored[t % 3], 16 * (t // 3))
                    link(dve.tensor_tensor_reduce(buf[:, t % 3, :], src(t), src(t), 1.0, 0.0, ALU.mult, ALU.add, ssq[:, t:t + 1]))
                    dve.tensor_scalar(rms[:, t:t + 1], ssq[:, t:t + 1], 1.0 / D, EPS, ALU.mult, ALU.add).then_inc(ns["meansq"], 1)

                def copy(t):
                    dve.wait_ge(ns["turned"], t + 1)
                    dve.tensor_tensor(dest(t), bank(2 * (t % 2), 2).rearrange("p (k n) -> p k n", k=KD),
                                      gain(t).rearrange("p (k o) -> p k o", o=1).to_broadcast([P, KD, P]), ALU.mult).then_inc(ns["copied"], 1)

                mean_square(0)
                for t in range(n_tiles):
                    dve.wait_ge(ns["root"], t + 1)
                    dve.reciprocal(rstd[:, t:t + 1], rms[:, t:t + 1]).then_inc(ns["rinv"], 1)
                    if t + 1 < n_tiles:
                        mean_square(t + 1)
                    if t >= 1:
                        copy(t - 1)
                copy(n_tiles - 1)

            def hT_tile(t):
                return hT[:, :, t * P:(t + 1) * P]

            dve.wait_ge(setup["vecT_made"], 1)
            dve.tensor_copy(vecT[:, :], bank(4)[:, 0:P]).then_inc(setup["vecT_copied"], 1)
            dve.tensor_copy(b1T[:, :], bank(5)).then_inc(setup["vecT_copied"], 1)
            dve.tensor_copy(b2T[:, :], bank(6)[:, 0:2 * P]).then_inc(setup["vecT_copied"], 1)
            dve.wait_ge(setup["vecT_copied"], 3)
            b1e = b1T[:, :].rearrange("p (e g m) -> p e g m", e=E, g=2)
            link(dve.tensor_scalar(b1e[:, :, 1, :], b1e[:, :, 1, :], 1.0, None, ALU.add))
            dve.memset(mixg[:, :], 1.0)
            link(dve.memset(lam[:, 4:6], 0.0))
            link(dve.tensor_scalar(mixg[:, 0:DIFF_HEADS], vecT[:, G_SUB:G_SUB + 1].to_broadcast([P, DIFF_HEADS]),
                                   1.0 - LAM_INIT, None, ALU.mult))
            dve.wait_ge(setup["lam_in"], 64)
            for a in range(2):
                dve.tensor_tensor_reduce(lamv[:, 2 * a, :], lamv[:, 2 * a, :], lamv[:, 2 * a + 1, :], 1.0, 0.0,
                                         ALU.mult, ALU.add, lam[:, a:a + 1]).then_inc(setup["lam_dots"], 1)

            def ready0(t):
                if t < NT:
                    dve.wait_ge(x_in[t], 16)
                elif t == NT:
                    dve.wait_ge(setup["mem_in"], 16)

            norm_dve(norms[0], lambda t: xres[:, t, :] if t < NT else mrows[:, t - NT, :], xn, NT + 2,
                     lambda t: hT_tile(t) if t < NT else memT[:, :, (t - NT) * P:(t - NT + 1) * P],
                     lambda t: vecT[:, G_MIX:G_MIX + KD] if t < NT else vecT[:, G_MEMKV:G_MEMKV + KD], ready0)
            dve.wait_ge(setup["lam_exp"], 1)
            link(dve.tensor_tensor(lam[:, 4:5], lam[:, 3:4], lam[:, 2:3], ALU.subtract))
            link(dve.tensor_scalar(lam[:, 4:5], lam[:, 4:5], -LAM_INIT, None, ALU.add))
            neg_lam = lam[:, 4:5]

            dve.wait_ge(setup["alibi_made"], 1)
            link(dve.scalar_tensor_tensor(out=alibi, in0=alibi, scalar=-1.0, in1=alibi, op0=ALU.mult, op1=ALU.min))
            with dve.Fori(0, DIFF_HEADS) as i:
                link.enter(i, 1 + 16 + 16)
                link(dve.tensor_scalar(alibi, alibi, 0.25, None, ALU.mult))

                def add_bias(t):
                    for c2 in range(2):
                        a = 2 * (t % 2) + c2
                        if t >= 2:
                            dve.wait_ge(diff["comb"], i * 8 + t - 1)
                        dve.wait_ge(diff["scores"], i * 16 + 2 * t + c2 + 1)
                        carried(dve)
                        at = 896 - P * t
                        link(dve.tensor_tensor_reduce(sp[:, a, :], bank(2 * c2, 2), alibi[:, at:at + S], 1.0, LOWEST,
                                                      ALU.add, ALU.max, rmax[:, a:a + 1]))
                        dve.tensor_scalar(nmax[:, a:a + 1], rmax[:, a:a + 1], -1.0, None, ALU.mult).then_inc(diff["biased"], 1)

                def combine(t):
                    a = 2 * (t % 2)
                    dve.wait_ge(diff["exp"], i * 16 + 2 * t + 2)
                    if t >= 2:
                        dve.wait_ge(diff["squared"], i * 8 + t - 1)
                    link(dve.reciprocal(rinv[:, a:a + 2], rsum[:, a:a + 2]))
                    link(dve.tensor_scalar(coef[:, t % 2:t % 2 + 1], rsum[:, a:a + 1], rinv[:, a + 1:a + 2], neg_lam, ALU.mult, ALU.mult))
                    if t >= 1:
                        dve.wait_ge(diff["turned"], i * 8 + t)
                    dve.scalar_tensor_tensor(out=acomb, in0=sp[:, a + 1, :], scalar=coef[:, t % 2:t % 2 + 1], in1=sp[:, a, :],
                                             op0=ALU.mult, op1=ALU.add).then_inc(diff["comb"], 1)

                def normalise(t):
                    dve.wait_ge(diff["out"], i * 8 + t + 1)
                    dve.tensor_scalar(mix[:, t, bass.ds(i * P, P)], bank(6 + t % 2)[:, 0:P],
                                      rinv[:, 2 * (t % 2):2 * (t % 2) + 1], None, ALU.mult).then_inc(diff["out_copied"], 1)

                for t in range(NT):
                    add_bias(t)
                    if t >= 2:
                        normalise(t - 2)
                    if t >= 1:
                        combine(t - 1)
                normalise(NT - 2)
                combine(NT - 1)
                normalise(NT - 1)
                dve.wait_ge(diff["squared"], i * 8 + 8)
                dve.tensor_scalar(sub_ms[:, bass.ds(i * NT, NT)], ssq8, 1.0 / P, EPS, ALU.mult, ALU.add).then_inc(diff["meansq"], 1)
                link.leave(DIFF_HEADS)

            dve.wait_ge(setup["small_in"], 32)
            dve.wait_ge(setup["pads_zero"], 1)
            rows_all = 2 * NA_TABLE // GRID_W
            with dve.Fori(0, NA_PAIRS) as i:
                link.enter(i, 1 + 4 + 16 + 16)
                dve.wait_ge(na["tab_in"], i * 16 + 16)
                tab_rows = tables.rearrange("p (r c) -> p r c", c=GRID_W)
                link(dve.tensor_tensor(tab_rows, tab_rows, cmask.rearrange("p (o c) -> p o c", o=1)
                                       .to_broadcast([P, rows_all, GRID_W]), ALU.add))
                for c2 in range(2):
                    link(dve.memset(na_tab[0:HD, c2, NA_EDGE + NA_ROWS * GRID_W:NA_TABLE], NEG))
                    link(dve.memset(na_tab[HD:P, c2, NA_EDGE:NA_EDGE + GRID_W], NEG))

                def add_bias(u):
                    t, c2 = divmod(u, 2)
                    _, width, at = na_window(t)
                    if u >= 4:
                        dve.wait_ge(na["turned"], i * 16 + u - 3)
                    dve.wait_ge(na["scores"], i * 16 + u + 1)
                    carried(dve)
                    link(dve.tensor_tensor_reduce(sp[:, u % 4, 0:width], bank(2 * (u % 2), 2)[:, 0:width],
                                                  na_tab[:, c2, at:at + width], 1.0, LOWEST, ALU.add, ALU.max,
                                                  rmax[:, u % 4:u % 4 + 1]))
                    dve.tensor_scalar(nmax[:, u % 4:u % 4 + 1], rmax[:, u % 4:u % 4 + 1], -1.0, None, ALU.mult).then_inc(na["biased"], 1)

                def normalise(u):
                    t, c2 = divmod(u, 2)
                    dve.wait_ge(na["out"], i * 16 + u + 1)
                    link(dve.reciprocal(rinv[:, u % 4:u % 4 + 1], rsum[:, u % 4:u % 4 + 1]))
                    dve.tensor_scalar(mix[:, t, bass.ds(HALF + c2 * HD + i * P, HD)], bank(6 + u % 2)[:, 0:HD],
                                      rinv[:, u % 4:u % 4 + 1], None, ALU.mult).then_inc(na["out_copied"], 1)

                for u in range(16):
                    add_bias(u)
                    if u >= 3:
                        normalise(u - 3)
                for u in range(13, 16):
                    normalise(u)
                link.leave(NA_PAIRS)

            dve.wait_ge(mixed["root"], 1)
            link(dve.reciprocal(sub_rs, sub_ms))
            for t in range(NT):
                v = mix[:, t, 0:DIFF_HEADS * P].rearrange("p (h v) -> p h v", h=DIFF_HEADS)
                dve.tensor_tensor(v, v, sub_rs.rearrange("p (h t o) -> p h t o", h=DIFF_HEADS, o=1)[:, :, t, :]
                                  .to_broadcast([P, DIFF_HEADS, P]), ALU.mult).then_inc(mixed["scaled"], 1)
                if t >= 1:
                    mix_copy(dve, t - 1)
            mix_copy(dve, NT - 1)
            for t in range(NT):
                dve.wait_ge(mixed["made"], t + 1)
                dve.tensor_tensor(xres[:, t, :], xres[:, t, :], bank(4 + 2 * (t % 2), 2), ALU.add).then_inc(mixed["added"], 1)
            norm_dve(norms[1], lambda t: xres[:, t, :], xn2, NT, hT_tile, lambda t: vecT[:, G_MEMQ:G_MEMQ + KD],
                     lambda t: dve.wait_ge(mixed["added"], t + 1))

            def cross_add(t):
                dve.wait_ge(cross["made"], t + 1)
                for n in range(2):
                    o = xres[:, t, n * HALF:(n + 1) * HALF]
                    dve.tensor_tensor(o, o, bank(4 + n), ALU.add).then_inc(cross["added"], 1)

            for t in range(NT):
                dve.wait_ge(cross["scores"], t + 1)
                if t >= 1:
                    dve.wait_ge(cross["exp"], t)
                link(dve.tensor_reduce(cross_max, bank(2 * (t % 2), 2)
                                       .rearrange("p (h n) -> p h n", h=MH), AX.X, ALU.max))
                dve.tensor_scalar(nmax, cross_max, -1.0, None, ALU.mult).then_inc(cross["max"], 1)
                dve.wait_ge(cross["exp"], t + 1)
                link(dve.reciprocal(rinv, rsum))
                dve.wait_ge(cross["out"], t + 1)
                dve.tensor_tensor(om.rearrange("p (h d) -> p h d", h=MH), bank(6)[:, 0:MEM].rearrange("p (h d) -> p h d", h=MH),
                                  rinv.rearrange("p (h o) -> p h o", o=1).to_broadcast([P, MH, HD]), ALU.mult).then_inc(cross["out_copied"], 1)
                cross_add(t)
            norm_dve(norms[2], lambda t: xres[:, t, :], xn2, NT, hT_tile, lambda t: vecT[:, G_FFN:G_FFN + KD],
                     lambda t: dve.wait_ge(cross["added"], 2 * t + 2))

            def per_tile(ap):
                return ap.rearrange("p (t e) -> p t e", t=NT)

            dve.wait_ge(route["logits"], 1)
            dve.wait_ge(route["consts"], 2)
            link(dve.tensor_tensor(logit, per_tile(bank(4)[:, 0:NT * E]), brt[:, :].rearrange("p (o e) -> p o e", o=1)
                                   .to_broadcast([P, NT, E]), ALU.add))
            for t in range(NT):
                last = dve.max(top8[:, t, :], logit[:, t, :])
            link(last)
            for t in range(NT):
                last = dve.max_index(top8i[:, t, :], top8[:, t, :], logit[:, t, :])
            link(last)
            chosen = prod[:, 0, 0:NT * TOPK].rearrange("p (t k) -> p t k", t=NT)
            link(dve.tensor_copy(chosen, top8i[:, :, 0:TOPK]))
            for k in range(TOPK):
                last = dve.tensor_tensor(per_tile(oneh[:, k, :]), iota_e.rearrange("p (o e) -> p o e", o=1).to_broadcast([P, NT, E]),
                                         chosen[:, :, k:k + 1].to_broadcast([P, NT, E]), ALU.is_equal)
            link(last)
            link(dve.tensor_tensor(msum, oneh[:, 0, :], oneh[:, 1, :], ALU.add))
            link(dve.tensor_tensor(msum, msum, oneh[:, 2, :], ALU.add))
            dve.tensor_tensor(msum, msum, oneh[:, 3, :], ALU.add).then_inc(route["masked"], 1)
            dve.tensor_tensor(gates[:, :, :], top8[:, :, 0:TOPK], top8[:, :, 0:1].to_broadcast([P, NT, TOPK]),
                              ALU.subtract).then_inc(route["gate_in"], 1)
            dve.wait_ge(route["placed"], 1)
            link(dve.tensor_copy(cnt[:, 0:E], bank(6)[:, 0:E]))
            dve.tensor_reduce(cnt[:, E:E + 1], cnt[:, 0:E], AX.X, ALU.max).then_inc(route["cnt_made"], 1)
            link(dve.scalar_tensor_tensor(out=slotm, in0=bank(5)[:, 0:NT * E], scalar=float(EC),
                                          in1=iota_e.rearrange("p (o e) -> p o e", o=1).to_broadcast([P, NT, E]),
                                          op0=ALU.mult, op1=ALU.add))
            for k in range(TOPK):
                link(dve.tensor_tensor(prod[:, k % 2, :], oneh[:, k, :], slotm, ALU.mult))
                link(dve.tensor_reduce(slot_f[:, k, :], per_tile(prod[:, k % 2, :]), AX.X, ALU.add))
            dve.tensor_scalar(slot_u[:, :, :], slot_f[:, :, :], 1.0, None, ALU.add).then_inc(route["slots"], 1)
            dve.wait_ge(route["gate_exp"], 1)
            gsum = st[:, 58:58 + NT]
            link(dve.tensor_reduce(gsum, gates[:, :, :], AX.X, ALU.add))
            link(dve.reciprocal(gsum, gsum))
            dve.tensor_tensor(gates[:, :, :], gates[:, :, :], gsum.rearrange("p (t o) -> p t o", o=1)
                              .to_broadcast([P, NT, TOPK]), ALU.mult).then_inc(route["gates_made"], 1)

            dve.wait_ge(route["idx_in"], 48)
            link(dve.tensor_scalar(token_all, choice_all, int(math.log2(TOPK)), None, ALU.logical_shift_right))
            dve.sem_inc(route["tokens_made"], 1)

            def x_copy(ns, n, cols=CAP):
                for q in range(4):
                    dve.wait_ge(ns["x_turned"], n * 4 + q + 1)
                    dve.tensor_tensor(xT[:, 2 * q:2 * q + 2, 0:cols], bank(4 + q % 2)[:, 0:2 * CAP].rearrange("p (k n) -> p k n", k=2)[:, :, 0:cols],
                                      vecT[:, G_FFN + 2 * q:G_FFN + 2 * q + 2].rearrange("p (k o) -> p k o", o=1)
                                      .to_broadcast([P, 2, cols]), ALU.mult).then_inc(ns["x_copied"], 1)

            def gate_up(ns, n, e):
                def finish(m):
                    dve.wait_ge(ns["sig"], n * 8 + m + 1)
                    link(dve.tensor_tensor(ep[:, m % 2, 3, :], ep[:, m % 2, 0, :], ep[:, m % 2, 2, :], ALU.mult))
                    dve.scalar_tensor_tensor(out=actT[:, m, :], in0=ep[:, m % 2, 1, :], scalar=1.0 - LIMIT,
                                             in1=ep[:, m % 2, 3, :], op0=ALU.max, op1=ALU.mult).then_inc(ns["act"], 1)

                for m in range(KF):
                    if m >= 2:
                        dve.wait_ge(ns["act"], n * 8 + m - 1)
                    dve.wait_ge(ns["up"], n * 8 + m + 1)
                    dve.tensor_scalar(ep[:, m % 2, 1, :], bank(m % 2)[:, CAP:2 * CAP], b1T[:, bass.ds(e * 16 + 8 + m, 1)],
                                      1.0 + LIMIT, ALU.add, ALU.min)
                    dve.tensor_scalar(ep[:, m % 2, 0, :], bank(m % 2)[:, 0:CAP], b1T[:, bass.ds(e * 16 + m, 1)],
                                      LIMIT, ALU.add, ALU.min).then_inc(ns["gated"], 1)
                    if m >= 1:
                        finish(m - 1)
                finish(KF - 1)
                dve.wait_ge(ns["act"], n * 8 + 8)
                carried(dve)

            for stage in (moe, over):
                dve.sem_inc(stage["x_copied"], PRIMED)
            dve.wait_ge(final["cleared"], 2)
            x_copy(moe, 0)
            with dve.Fori(0, E) as e:
                link.enter(e, 8)
                gate_up(moe, e, e)
                x_copy(moe, e + 1)
                link.leave(E)
            most = dve.value_load(cnt[0:1, E:E + 1], min_val=0, max_val=S)
            over_base = link.base
            with dve.If(most > CAP):
                with dve.Fori(0, E) as e:
                    n = dve.value_load(cnt[0:1, bass.ds(e, 1)], min_val=0, max_val=S)
                    for j in range(N_OVER):
                        item = e * N_OVER + j
                        with dve.If(n > CAP + j * OVER):
                            link.base, link.n = over_base, 0
                            link.enter(item, 8)
                            x_copy(over, item, OVER)
                            gate_up(over, item, e)
                            dve.wait_ge(over["act"], item * 8 + 8)
                            carried(dve)
                            link.leave(0)
                        with dve.Else():
                            dve.sem_inc(dve_link, 8)
                            for s, v in ((over["x_copied"], 4), (over["gated"], 8), (over["act"], 8)):
                                dve.sem_inc(s, v)
                        dve.nop()
            with dve.Else():
                dve.sem_inc(dve_link, 8 * E * N_OVER)
            link.base, link.n = over_base + 8 * E * N_OVER, 0

            dve.wait_ge(final["g_in"], 16)
            dve.wait_ge(moe["y_copied"], 8 * E + PRIMED)

            def finish_tile(t):
                dve.wait_ge(final["root"], t + 1)
                link(dve.reciprocal(rstd[:, t:t + 1], rms[:, t:t + 1]))
                dve.scalar_tensor_tensor(out=facc[:, t, :], in0=xres[:, t, :], scalar=rstd[:, t:t + 1], in1=gfin,
                                         op0=ALU.mult, op1=ALU.mult).then_inc(final["scaled"], 1)

            for t in range(NT):
                dve.wait_ge(final["rows_in"][t % 2], 16 * (t // 2 + 1))
                for k in range(TOPK):
                    ins = dve.scalar_tensor_tensor(out=xres[:, t, :], in0=yg[:, (t % 2) * TOPK + k, :], scalar=gates[:, t, k:k + 1],
                                                   in1=xres[:, t, :], op0=ALU.mult, op1=ALU.add)
                    if k < TOPK - 1:
                        link(ins)
                    else:
                        ins.then_inc(final["sum"], 1)
                dve.wait_ge(final["sum"], t + 1)
                link(dve.tensor_tensor_reduce(facc[:, t, :], xres[:, t, :], xres[:, t, :], 1.0, 0.0, ALU.mult, ALU.add, ssq[:, t:t + 1]))
                dve.tensor_scalar(rms[:, t:t + 1], ssq[:, t:t + 1], 1.0 / D, EPS, ALU.mult, ALU.add).then_inc(final["squares"], 1)
                if t >= 1:
                    finish_tile(t - 1)
            finish_tile(NT - 1)

        def mix_copy(dve, t):
            dve.wait_ge(mixed["turned"], t + 1)
            dve.tensor_tensor(hT[:, :, t * P:(t + 1) * P], bank(2 * (t % 2), 2).rearrange("p (k n) -> p k n", k=KD),
                              mixg[:, :].rearrange("p (k o) -> p k o", o=1).to_broadcast([P, KD, P]), ALU.mult).then_inc(mixed["copied"], 1)

        block.vector(vector_program)


_INS = ["x", "mem", "norm_mix_g", "w_in", "lambda_q1", "lambda_k1", "lambda_q2", "lambda_k2", "subln_g", "rpb",
        "w_out", "norm_mem_q_g", "norm_mem_kv_g", "w_mq", "w_mkv", "w_mo", "norm_ffn_g", "w_router", "b_router",
        "w1", "b1", "w2", "b2", "norm_final_g"]


def column_mask():
    import numpy as np
    col = np.arange(2 * GRID_W) % GRID_W
    start = np.clip(col - NA_COLS // 2, 0, GRID_W - NA_COLS)
    key = np.arange(GRID_W)
    inside = (key[None] >= start[:, None]) & (key[None] < start[:, None] + NA_COLS)
    return np.where(inside, 0.0, NEG).astype(np.float32)


def kernel(**inputs):
    import numpy as np
    from concourse import bacc
    from concourse.bass_utils import run_bass_kernel_spmd

    nc = bacc.Bacc("TRN2", target_bir_lowering=False, num_devices=1)
    arrays, args = {}, []
    for name in _INS + ["col_mask"]:
        a = column_mask() if name == "col_mask" else np.ascontiguousarray(inputs[name])
        arrays[f"in_{name}"] = a
        args.append(nc.dram_tensor(f"in_{name}", a.shape, mybir.dt.from_np(a.dtype), kind="ExternalInput").ap())
    args.append(nc.dram_tensor("out_y", (1, S, D), F32, kind="ExternalOutput").ap())
    encoder_layer(nc, *args)
    r = run_bass_kernel_spmd(nc, [arrays], core_ids=[0])
    return r.results[0]["out_y"]
```

```python
import math
from contextlib import ExitStack

import concourse.bass as bass
from concourse import mybir

F32 = mybir.dt.float32
F32R = mybir.dt.float32r
U32 = mybir.dt.uint32
I32 = mybir.dt.int32
ALU = mybir.AluOpType
ACT = mybir.ActivationFunctionType
AX = mybir.AxisListType

P = 128
D = 1024
S = 1024
KD = D // P
NT = S // P
HALF = 512
HD = 64
DIFF_HEADS = 4
NA_PAIRS = 4
GRID_W = 64
NA_ROWS, NA_COLS = 8, 16
RPB_R, RPB_C = 2 * NA_ROWS - 1, 2 * NA_COLS - 1
RPB_HEAD = RPB_R * RPB_C
RPB_PAD = 64
RPB_LEN = 3840 + 2 * RPB_PAD
MEM = 256
MH = 4
E = 32
TOPK = 4
FF = 1024
KF = FF // P
EPS = 1e-5
LIMIT = 7.0
ALPHA = 1.702
LAM_INIT = 0.8 - 0.6 * math.exp(-0.3 * 0)
QSCALE = 1.0 / math.sqrt(HD)
NEG = -1.0e30
LOWEST = -3.0e38

CAP = 192
CAP2 = CAP - P
OVER = 128
N_OVER = -(-(S - CAP) // OVER)
POSN = CAP + N_OVER * OVER
EC = E + 2
NOBODY = 1 << 20
VARIANTS = (64, *range(88, CAP + 1, 8))

PRIMED = 8

COPIES, SPLITS = 14, 12

G_MIX, G_MEMQ, G_MEMKV, G_FFN, G_SUB = 0, 8, 16, 24, 32


class Link:

    def __init__(self, eng, sem):
        self.eng, self.sem, self.base, self.n, self.it, self.per = eng, sem, 0, 0, None, 0

    def mark(self, ins):
        self.n += 1
        ins.then_inc(self.sem, 1)
        at = self.base + self.n
        return at if self.it is None else self.it * self.per + at

    def need(self, value):
        self.eng.wait_ge(self.sem, value)

    def __call__(self, ins):
        self.need(self.mark(ins))

    def enter(self, it, per):
        self.base += self.n
        self.n, self.it, self.per = 0, it, per

    def leave(self, trips):
        assert self.n == self.per, (self.n, self.per)
        self.base += trips * self.per
        self.n, self.it = 0, None


def stage_sems(sem, stage, names):
    return {n: sem(f"{stage}_{n}") for n in names.split()}


def na_window(t):
    r = 2 * t
    lo = min(max(r - NA_ROWS // 2, 0), S // GRID_W - NA_ROWS)
    hi = min(max(r + 1 - NA_ROWS // 2, 0), S // GRID_W - NA_ROWS)
    if lo == hi:
        return lo * GRID_W, NA_ROWS * GRID_W, (lo - r + NA_ROWS - 1 - 1) * GRID_W
    return lo * GRID_W, (NA_ROWS + 1) * GRID_W, NA_EDGE


def na_place(width):
    return (0, width) if width <= HALF else (HALF - width // 2, width // 2)


NA_EDGE = 14 * GRID_W
NA_TABLE = NA_EDGE + (NA_ROWS + 1) * GRID_W


def encoder_layer(nc, x, mem, norm_mix_g, w_in, lambda_q1, lambda_k1, lambda_q2, lambda_k2, subln_g, rpb,
                  w_out, norm_mem_q_g, norm_mem_kv_g, w_mq, w_mkv, w_mo, norm_ffn_g, w_router, b_router,
                  w1, b1, w2, b2, norm_final_g, col_mask, out):
    ctx = ExitStack()
    with ctx:
        def sb(name, shape, dt=F32):
            return ctx.enter_context(nc.sbuf_tensor(name, shape, dt))

        def sem(name):
            return ctx.enter_context(nc.semaphore(name))

        rpb_pad = nc.dram_tensor("rpb_pad", [RPB_LEN], F32, kind="Internal").ap()
        na_bias = nc.dram_tensor("na_bias", [2 * NA_PAIRS, P, NA_TABLE], F32, kind="Internal").ap()
        h_rows = nc.dram_tensor("h_rows", [S, D], F32, kind="Internal").ap()
        slot_choice = nc.dram_tensor("slot_choice", [POSN * EC, 1], U32, kind="Internal").ap()
        y_rows = nc.dram_tensor("y_rows", [S * TOPK, D], F32, kind="Internal").ap()

        xres = sb("xres", [P, NT, D])
        hT = sb("hT", [P, KD, S])
        with nc.sbuf_tensor("q_parts", [P, 2, S], F32R) as q_parts, nc.sbuf_tensor("k_high", [P, 2, S], F32R) as k_high, \
                nc.sbuf_tensor("k_low", [P, 2, S], F32R) as k_low:
            pass
        arena = sb("arena", [P, 3 * 8192])
        work_len = 9088 + 256
        work = sb("work", [P, work_len])
        ident = sb("ident", [P, P])
        vecT = sb("vecT", [P, P])
        mixg = sb("mixg", [P, KD])
        b1T = sb("b1T", [P, 4 * P])
        b2T = sb("b2T", [P, 2 * P])
        kmz = sb("kmz", [P, 2, 2, MEM])
        vmem = sb("vmem", [P, 2, MEM])
        minus_half = sb("minus_half", [P, DIFF_HEADS * NT])
        st = sb("st", [P, 96])
        PS = ctx.enter_context(nc.psum_tensor("PS", [P, 8, HALF], F32))

        def bank(b, n=1):
            return PS[:, b:b + n, :].rearrange("p a b -> p (a b)")

        def carver(region, total):
            at = [0]

            def carve(size, pattern=None, **kw):
                a = region[:, at[0]:at[0] + size]
                at[0] += size
                assert at[0] <= total, (at[0], total)
                return a.rearrange(pattern, **kw) if pattern else a
            return carve

        r0, r1, r2 = (arena[:, i * 8192:(i + 1) * 8192] for i in range(3))
        wA = r0.rearrange("p (k g n) -> p k g n", k=KD, g=2)
        wB = r1.rearrange("p (k g n) -> p k g n", k=KD, g=2)
        wD = r2.rearrange("p (k n) -> p k n", k=KF)
        c = carver(r0, 8192)
        wmkv = c(4096, "p (k n) -> p k n", k=KD)
        memT = c(2048, "p (k n) -> p k n", k=KD)
        mrows = c(2048, "p (a n) -> p a n", a=2)
        c = carver(r2, 8192)
        vrows = c(P)
        brows = c(6 * P, "p (a n) -> p a n", a=6)
        lamv = c(4 * HD, "p (a n) -> p a n", a=4)
        mix = r2.rearrange("p (t n) -> p t n", t=NT)
        c = carver(r1, 8192)
        wqkv = c(3 * KD * P, "p (j k n) -> p j k n", j=3, k=KD)
        wout_c = c(D)
        xn = c(3 * D, "p (a n) -> p a n", a=3)
        pT2 = xn[:, 0:2, :]
        acomb = xn[:, 2, :]
        v_sb = c(S, "p (t n) -> p t n", t=NT)
        c = carver(work, work_len)
        wout_a = c(2 * D, "p (k n) -> p k n", k=2)
        sp = c(4 * D, "p (a n) -> p a n", a=4)
        tables = c(2 * NA_TABLE)
        na_tab = tables.rearrange("p (a n) -> p a n", a=2)
        alibi = tables[:, 0:1920]
        junk = c(P)
        sub_ms = c(DIFF_HEADS * NT)
        sub_rs = c(DIFF_HEADS * NT)
        cmask = c(GRID_W)
        wout_late = r0[:, 0:3 * D].rearrange("p (k n) -> p k n", k=3)
        wout_b = r0[:, 6 * D:8 * D].rearrange("p (k n) -> p k n", k=2)
        wout = [wout_a[:, 0, :], wout_a[:, 1, :], wout_b[:, 0, :], wout_b[:, 1, :], wout_c] + [wout_late[:, k, :] for k in range(3)]
        c = carver(r1, 8192)
        wmq = c(2048, "p (k n) -> p k n", k=KD)
        c(2048)
        wmo = c(2048, "p (k n) -> p k n", k=2)
        c = carver(work, work_len)
        qmT = c(2 * S, "p (a n) -> p a n", a=2)
        mp = c(2 * D, "p (a n) -> p a n", a=2)
        mpT = c(D)
        om = c(MEM)
        omT = c(MEM)
        xn2 = c(3 * D, "p (a n) -> p a n", a=3)
        wrt = c(KD * E, "p (k n) -> p k n", k=KD)
        c = carver(r2, 8192)
        logit = c(2 * E, "p (a e) -> p a e", a=2)
        oneh = c(2 * TOPK * E, "p (a k e) -> p a k e", a=2, k=TOPK)
        prod = c(TOPK * E, "p (k e) -> p k e", k=TOPK)
        msum = c(NT * E)
        slotm = c(E)
        ones = c(P)
        before = c(P)
        iota_e = c(E)
        top8 = c(NT * 8, "p (t k) -> p t k", t=NT)
        top8i = c(NT * 8).bitcast(U32).rearrange("p (t k) -> p t k", t=NT)
        chosen = c(NT * TOPK, "p (t k) -> p t k", t=NT)
        slot_f = c(NT * TOPK, "p (t k) -> p t k", t=NT)
        c = carver(work, work_len)
        xg = c(2 * D, "p (a n) -> p a n", a=2)
        actT = c(KF * CAP, "p (k n) -> p k n", k=KF)
        yT = c(KD * CAP, "p (k n) -> p k n", k=KD)
        c = carver(hT[:, :, :].rearrange("p k n -> p (k n)"), 8192)
        xT = c(KD * CAP, "p (k n) -> p k n", k=KD)
        ysb = c(2 * D, "p (a n) -> p a n", a=2)
        ep = c(8 * CAP, "p (b j n) -> p b j n", b=2, j=4)
        idx_now = c(4).bitcast(U32)
        choice_all = c((2 + N_OVER) * EC).bitcast(U32)
        token_all = c((2 + N_OVER) * EC).bitcast(U32)

        def place_tables(table):
            return (table[:, 0:EC], table[0:CAP2, EC:2 * EC],
                    table[:, 2 * EC:].rearrange("p (j c) -> p j c", j=N_OVER))

        choice_a, choice_b, choice_o = place_tables(choice_all)
        token_a, token_b, token_o = place_tables(token_all)
        gfin = r0[:, 0:D]
        yg = [(r1 if a < 8 else work)[:, (a % 8) * D:(a % 8 + 1) * D] for a in range(16)]
        facc = r2.rearrange("p (a n) -> p a n", a=8)
        cnt = sb("cnt", [P, E + 1], I32)
        gates = sb("gates", [P, NT, TOPK])
        slot_u = sb("slot_u", [P, NT, TOPK], U32)
        choice = sb("choice", [P, NT, TOPK], U32)
        brt = sb("brt", [P, E])

        ssq, rstd = st[:, 0:10], st[:, 20:30]
        nmax, rsum, rinv = st[:, 30:34], st[:, 34:38], st[:, 38:42]
        lam = st[:, 44:50]
        coef = st[:, 42:44]
        rmax = st[:, 74:78]
        ssq8 = st[:, 50:58]
        rinv8 = st[:, 80:88]
        cross_max = st[:, 70:74]
        rsum8 = st[:, 88:96]

        tile_in = [sem(f"tile_in{t}") for t in range(NT)]
        setup = stage_sems(sem, "setup", "vec_cleared vec_in lam_in mem_in wmkv_in rpb_zero rpb_in bias_made small_in "
                 "vecT_made vecT_copied mkv_made mkv_copied alibi_made lam_dots lam_exp ident_made pads_zero kz_zero")
        norms = [stage_sems(sem, f"norm{i}", "squared rinv scaled turned copied") for i in range(3)]
        na = stage_sems(sem, "na", "w_in tab_in proj proj_copied split scores biased exp turned turned_copied out out_copied")
        diff = stage_sems(sem, "diff", "w_in proj proj_copied split scores biased exp comb turned turned_copied out out_copied squared meansq")
        mixed = stage_sems(sem, "mix", "wout_in sub_rinv scaled turned copied made added")
        cross = stage_sems(sem, "cross", "wmq_in wmo_in q q_copied scores max exp turned turned_copied out out_copied "
                  "out_turned out_turned_copied made added")
        route = stage_sems(sem, "route", "w_in logits masked placed counted slots gate_in gate_exp table_clear scattered "
                  "idx_in tokens_made cnt_made gates_made consts")
        moe = stage_sems(sem, "moe", "rows_free picked wA_in wB_in wD_in gathered x_turned x_copied up gated sig act down y_copied "
                  "y_turned y_moved named stored")
        over = stage_sems(sem, "over", "picked wA_in wB_in wD_in gathered x_turned x_copied up gated sig act down y_copied "
                  "y_turned y_moved named stored idle")
        final = stage_sems(sem, "final", "g_in sum squared rinv scaled_act gained scaled stored cleared")
        h_stored = [sem(f"h_stored{a}") for a in range(3)]
        dve_link, pool_link = sem("dve_link"), sem("pool_link")
        wait_passed = sem("wait_passed")

        POOL_TILES = NT - 2

        def by_pool(t):
            return t < POOL_TILES

        def carried(eng):
            eng.sem_inc(wait_passed, 1)

        block = ctx.enter_context(nc.Block())

        @block.sync
        def _(sp_):
            sp_.dma_start(mrows[:, :, :], mem[0].rearrange("(a p) n -> p a n", p=P)).then_inc(setup["mem_in"], 16)

            def load_x(t):
                sp_.dma_start(xres[:, t, :], x[0, t * P:(t + 1) * P, :]).then_inc(tile_in[t], 16)

            load_x(0)
            load_x(1)
            sp_.wait_ge(setup["vec_cleared"], 1)
            for row, g in ((G_MIX, norm_mix_g), (G_MEMQ, norm_mem_q_g), (G_MEMKV, norm_mem_kv_g), (G_FFN, norm_ffn_g)):
                sp_.dma_start(vrows[row:row + KD, :], g[0, :].rearrange("(c p) -> c p", p=P)).then_inc(setup["vec_in"], 16)
            sp_.dma_start(vrows[G_SUB:G_SUB + 1, :], subln_g[0:1, :]).then_inc(setup["vec_in"], 16)
            sp_.dma_start(brows[:, 0:4, :], b1[0].rearrange("e (f p) -> (e f) p", p=P)
                          .rearrange("(c r) p -> r c p", r=P)).then_inc(setup["vec_in"], 16)
            sp_.dma_start(brows[:, 4:6, :], b2[0].rearrange("e (f p) -> (e f) p", p=P)
                          .rearrange("(c r) p -> r c p", r=P)).then_inc(setup["vec_in"], 16)
            for t in range(2, 5):
                load_x(t)
            sp_.dma_start(wmkv[:, :, :], w_mkv[0].rearrange("(k p) n -> p k n", p=P)).then_inc(setup["wmkv_in"], 16)
            for t in range(5, NT):
                load_x(t)
            sp_.wait_ge(setup["rpb_zero"], 16)
            sp_.dma_start(rpb_pad[RPB_PAD:RPB_PAD + 8 * RPB_HEAD], rpb[0].rearrange("h r c -> (h r c)")).then_inc(setup["rpb_in"], 16)

            def load_head(base, i, s, j0=0):
                for j, first in enumerate(base):
                    sp_.dma_start(wqkv[:, j, :, :], w_in[0, :, bass.ds(first + i * P, P)]
                                  .rearrange("(k p) n -> p k n", p=P)).then_inc(s, 16)

            def spread_bias(q):
                for half in range(2):
                    for first, n, low in ((0, 14, 1), (NA_EDGE, NA_ROWS + 1, 3)):
                        start = RPB_PAD + (low - half) * RPB_C + NA_COLS - 1
                        src = rpb_pad[bass.ds(start - q, 2 * NA_PAIRS * RPB_HEAD)].rearrange("(h n) -> h n", h=2 * NA_PAIRS)[
                            :, 0:n * RPB_C].rearrange("h (r c) -> h r c", c=RPB_C)
                        src = bass.AP(tensor=src.tensor, offset=src.offset, ap=[[RPB_HEAD, 2 * NA_PAIRS], [RPB_C, n], [1, GRID_W]])
                        sp_.dma_start(na_bias[:, bass.ds(q + half * HD, 1), first:first + n * GRID_W]
                                      .rearrange("h a (r c) -> h (a r) c", r=n), src).then_inc(setup["bias_made"], 16)

            QS = GRID_W // DIFF_HEADS
            sp_.wait_ge(setup["rpb_in"], 16)
            load_head((0, 512, 1024), 0, diff["w_in"])
            sp_.wait_ge(setup["mkv_made"], 3)
            for rows, first in ((wout_a, 0), (wout_b, 2 * P)):
                sp_.dma_start(rows, w_out[0, first:first + 2 * P, :].rearrange("(k p) n -> p k n", p=P)).then_inc(mixed["wout_in"], 16)
            sp_.dma_start(wout_c, w_out[0, 4 * P:5 * P, :]).then_inc(mixed["wout_in"], 16)
            with sp_.Fori(0, QS) as q:
                spread_bias(q)
            with sp_.Fori(1, DIFF_HEADS) as i:
                sp_.wait_ge(diff["proj"], i * 6)
                load_head((0, 512, 1024), i, diff["w_in"])
                with sp_.Fori(0, QS) as q:
                    spread_bias(i * QS + q)

            def load_table(i):
                sp_.dma_start(na_tab, na_bias[bass.ds(i * 2, 2), :, :].rearrange("a p n -> p a n")).then_inc(na["tab_in"], 16)

            sp_.wait_ge(diff["proj"], 6 * DIFF_HEADS)
            load_head((1536, 2048, 2560), 0, na["w_in"])
            sp_.wait_ge(setup["bias_made"], 16 * 4 * GRID_W)
            sp_.wait_ge(diff["biased"], 16 * DIFF_HEADS)
            load_table(0)
            with sp_.Fori(1, NA_PAIRS) as i:
                sp_.wait_ge(na["proj"], i * 6)
                load_head((1536, 2048, 2560), i, na["w_in"])
                sp_.wait_ge(na["biased"], i * 16)
                load_table(i)
            sp_.wait_ge(na["scores"], 16 * NA_PAIRS)
            sp_.dma_start(wout_late, w_out[0, 5 * P:, :].rearrange("(k p) n -> p k n", p=P)).then_inc(mixed["wout_in"], 16)
            sp_.wait_ge(na["out"], 16 * NA_PAIRS)
            sp_.dma_start(wmq[:, :, :], w_mq[0].rearrange("(k p) n -> p k n", p=P)).then_inc(cross["wmq_in"], 16)
            sp_.dma_start(wmo[:, :, :], w_mo[0].rearrange("(k p) n -> p k n", p=P)).then_inc(cross["wmo_in"], 16)
            sp_.dma_start(wrt[:, :, :], w_router[0].rearrange("(k p) n -> p k n", p=P)).then_inc(route["w_in"], 16)

            def load_up(buf, first, e, s):
                for g in range(2):
                    sp_.dma_start(buf[:, :, g, :], w1[0, bass.ds(e, 1), :, g * FF + first:g * FF + first + HALF]
                                  .rearrange("a (k p) n -> p (a k) n", p=P)).then_inc(s, 16)

            def load_down(e, s):
                sp_.dma_start(wD[:, :, :], w2[0, bass.ds(e, 1), :, :].rearrange("a (k p) n -> p (a k) n", p=P)).then_inc(s, 16)

            sp_.wait_ge(mixed["made"], NT)
            load_up(wA, 0, 0, moe["wA_in"])
            for t in range(NT):
                sp_.wait_ge(norms[2]["scaled"], t + 1)
                sp_.dma_start(h_rows[t * P:(t + 1) * P, :], xn2[:, t % 3, :]).then_inc(h_stored[t % 3], 16)
            sp_.wait_ge(cross["made"], NT)
            load_up(wB, HALF, 0, moe["wB_in"])
            sp_.wait_ge(route["scattered"], 16 * TOPK * NT)
            sp_.dma_start(choice_a[:, :], slot_choice[0:P * EC, :].rearrange("(p c) o -> p (c o)", c=EC)).then_inc(route["idx_in"], 16)
            sp_.dma_start(choice_b[:, :], slot_choice[P * EC:CAP * EC, :].rearrange("(p c) o -> p (c o)", c=EC)).then_inc(route["idx_in"], 16)
            sp_.dma_start(choice_o[:, :, :], slot_choice[CAP * EC:POSN * EC, :].rearrange("(j p c) o -> p j (c o)", c=EC, p=OVER)).then_inc(route["idx_in"], 16)
            sp_.wait_ge(route["gates_made"], 1)
            sp_.wait_ge(moe["gathered"], 32)
            load_down(0, moe["wD_in"])
            with sp_.Fori(0, E - 1) as e:
                sp_.wait_ge(moe["up"], e * 8 + 4)
                load_up(wA, 0, e + 1, moe["wA_in"])
                sp_.wait_ge(moe["up"], e * 8 + 8)
                load_up(wB, HALF, e + 1, moe["wB_in"])
                sp_.wait_ge(moe["down"], e * 8 + 8)
                load_down(e + 1, moe["wD_in"])
            sp_.wait_ge(moe["down"], 8 * E)
            most = sp_.value_load(cnt[0:1, E:E + 1], min_val=0, max_val=S)
            with sp_.If(most > CAP):
                with sp_.Fori(0, E) as e:
                    n = sp_.value_load(cnt[0:1, bass.ds(e, 1)], min_val=0, max_val=S)
                    for j in range(N_OVER):
                        with sp_.If(n > CAP + j * OVER):
                            sp_.wait_ge(over["idle"], e * N_OVER + j + PRIMED)
                            load_up(wA, 0, e, over["wA_in"])
                            load_up(wB, HALF, e, over["wB_in"])
                            load_down(e, over["wD_in"])
                            item = e * N_OVER + j
                            for s, v in ((over["wA_in"], 32), (over["wB_in"], 32), (over["wD_in"], 16)):
                                sp_.wait_ge(s, item * v + v)
                            carried(sp_)
                        with sp_.Else():
                            sp_.sem_inc(over["wA_in"], 32)
                            sp_.sem_inc(over["wB_in"], 32)
                            sp_.sem_inc(over["wD_in"], 16)
                        sp_.nop()
                sp_.wait_ge(over["idle"], E * N_OVER + PRIMED)
            with sp_.Else():
                sp_.nop()
            sp_.dma_start(gfin, norm_final_g.rearrange("(a n) -> a n", a=1).to_broadcast([P, D])).then_inc(final["g_in"], 16)
            def load_rows(t):
                if t >= 4:
                    sp_.wait_ge(final["sum"], t - 3)
                buf = (r1 if t % 4 < 2 else work)[:, (t % 2) * TOPK * D:(t % 2 + 1) * TOPK * D]
                sp_.dma_start(buf, y_rows[t * P * TOPK:(t + 1) * P * TOPK, :].rearrange("(p k) n -> p (k n)", k=TOPK)
                              ).then_inc(tile_in[t], 16)

            sp_.wait_ge(moe["stored"], 32 * (E + 1))
            for t in range(4):
                load_rows(t)
            for t in range(NT):
                if t + 4 < NT:
                    load_rows(t + 4)
                sp_.wait_ge(final["gained"] if by_pool(t) else final["scaled"], t + 1 if by_pool(t) else t + 1 - POOL_TILES)
                sp_.dma_start(out[0, t * P:(t + 1) * P, :], facc[:, t, :]).then_inc(final["stored"], 16)
            sp_.wait_ge(final["stored"], 16 * NT)

        @block.gpsimd
        def _(pool):
            link = Link(pool, pool_link)
            pool.memset(vrows, 0.0).then_inc(setup["vec_cleared"], 1)
            pool.wait_ge(setup["vec_cleared"], 1)
            link(pool.memset(ident[:, :], 0.0))
            pool.affine_select(out=ident[:, :], in_=ident[:, :], compare_op=ALU.not_equal, fill=1.0, base=0,
                               pattern=[[-1, P]], channel_multiplier=1).then_inc(setup["ident_made"], 1)
            pool.wait_ge(setup["ident_made"], 1)
            link(pool.memset(sp[:, 0, 0:HD], 0.0))
            link(pool.memset(minus_half[:, :], -0.5))
            pool.dma_start(rpb_pad.rearrange("(p n) -> p n", p=P), sp[:, 0, 0:RPB_LEN // P]).then_inc(setup["rpb_zero"], 16)
            for a, vector in enumerate((lambda_q1, lambda_k1, lambda_q2, lambda_k2)):
                pool.dma_start(lamv[:, a, :], vector[0:1, :].to_broadcast([P, HD])).then_inc(setup["lam_in"], 16)
            pool.dma_start(brt[:, :], b_router[0:1, :].to_broadcast([P, E])).then_inc(setup["small_in"], 16)
            pool.dma_start(cmask, col_mask).then_inc(setup["small_in"], 16)

            def inverse_rms(ns, t):
                pool.wait_ge(ns["squared"], t + 1)
                link(pool.tensor_scalar(ssq[:, t:t + 1], ssq[:, t:t + 1], EPS, None, ALU.add))
                pool.tensor_tensor(rstd[:, t:t + 1], ssq[:, t:t + 1], minus_half[:, 0:1], ALU.pow).then_inc(ns["rinv"], 1)
                pool.wait_ge(ns["rinv"], t + 1)

            link(pool.memset(kmz[0:HD, 1, :, :], 0.0))
            pool.memset(kmz[HD:P, 0, :, :], 0.0).then_inc(setup["kz_zero"], 1)
            pool.wait_ge(setup["kz_zero"], 1)
            for t in range(NT + 2):
                inverse_rms(norms[0], t)
            pool.iota(alibi, pattern=[[-1, 1920]], base=896, channel_multiplier=1,
                      allow_small_or_imprecise_dtypes=True).then_inc(setup["alibi_made"], 1)
            pool.wait_ge(setup["alibi_made"], 1)
            link(pool.iota(choice[:, :, :], pattern=[[TOPK * P, NT], [1, TOPK]], base=0, channel_multiplier=TOPK))
            empty = sp[:, 1, 0:POSN * EC // P].bitcast(U32)
            link(pool.memset(empty, NOBODY))
            pool.dma_start(slot_choice.rearrange("(p c) o -> p (c o)", p=P), empty).then_inc(route["table_clear"], 16)
            pool.wait_ge(diff["meansq"], DIFF_HEADS)
            link(pool.tensor_scalar(sub_ms, sub_ms, EPS, None, ALU.add))
            pool.tensor_tensor(sub_rs, sub_ms, minus_half[:, :], ALU.pow).then_inc(mixed["sub_rinv"], 1)
            pool.wait_ge(mixed["sub_rinv"], 1)
            pool.wait_ge(diff["comb"], NT * DIFF_HEADS)
            pool.memset(sp[:, :, 576:640], 0.0).then_inc(setup["pads_zero"], 1)
            pool.wait_ge(setup["pads_zero"], 1)
            for t in range(NT):
                inverse_rms(norms[1], t)
            pool.wait_ge(mixed["turned"], NT)
            link(pool.memset(ones, 1.0))
            pool.affine_select(out=before, in_=ones, compare_op=ALU.is_gt, fill=0.0, base=0, pattern=[[1, P]],
                               channel_multiplier=-1).then_inc(route["consts"], 1)
            pool.wait_ge(route["consts"], 1)
            pool.iota(iota_e, pattern=[[1, E]], base=0, channel_multiplier=0,
                      allow_small_or_imprecise_dtypes=True).then_inc(route["consts"], 1)
            pool.wait_ge(route["consts"], 2)

            def scatter(t):
                pool.wait_ge(route["slots"], t + 1)
                for k in range(TOPK):
                    pool.indirect_dma_start(out=slot_choice, out_offset=bass.IndirectOffsetOnAxis(slot_u[:, t, k:k + 1], 0),
                                            in_=choice[:, t, k:k + 1], in_offset=None).then_inc(route["scattered"], 16)

            pool.wait_ge(route["table_clear"], 16)
            for t in range(NT):
                inverse_rms(norms[2], t)
                if t >= 4:
                    scatter(t - 4)
            pool.wait_ge(cross["out"], NT)
            pool.memset(xg[:, :, :], 0.0).then_inc(final["cleared"], 1)
            pool.wait_ge(final["cleared"], 1)
            pool.memset(yT[:, :, :], 0.0).then_inc(final["cleared"], 1)
            pool.wait_ge(final["cleared"], 2)
            for t in range(4, NT):
                scatter(t)
            for t3 in range(3):
                pool.wait_ge(h_stored[t3], 16 * len(range(t3, NT, 3)))

            def store(a, b, ns, n):
                pool.tensor_copy(idx_now[:, 2:3], a).then_inc(ns["named"], 1)
                if b is not None:
                    pool.wait_ge(ns["named"], 2 * n + 1)
                    pool.tensor_copy(idx_now[0:CAP2, 3:4], b).then_inc(ns["named"], 1)
                pool.wait_ge(ns["named"], n + 1 if b is None else 2 * n + 2)
                pool.wait_ge(ns["y_moved"], (2 * n + 2 if b is None else 4 * n + 4) + PRIMED)
                carried(pool)
                pool.indirect_dma_start(out=y_rows, out_offset=bass.IndirectOffsetOnAxis(idx_now[:, 2:3], 0), in_=ysb[:, 0, :],
                                        in_offset=None, bounds_check=S * TOPK - 1, oob_is_err=False).then_inc(ns["stored"], 16)
                if b is not None:
                    pool.indirect_dma_start(out=y_rows, out_offset=bass.IndirectOffsetOnAxis(idx_now[0:CAP2, 3:4], 0),
                                            in_=ysb[0:CAP2, 1, :], in_offset=None, bounds_check=S * TOPK - 1,
                                            oob_is_err=False).then_inc(ns["stored"], 16)

            def gather(a, b, ns, n):
                pool.tensor_copy(idx_now[:, 0:1], a).then_inc(ns["picked"], 1)
                if b is not None:
                    pool.wait_ge(ns["picked"], 2 * n + 1)
                    pool.tensor_copy(idx_now[0:CAP2, 1:2], b).then_inc(ns["picked"], 1)
                pool.wait_ge(ns["picked"], n + 1 if b is None else 2 * n + 2)
                carried(pool)
                pool.indirect_dma_start(out=xg[:, 0, :], out_offset=None, in_=h_rows,
                                        in_offset=bass.IndirectOffsetOnAxis(idx_now[:, 0:1], 0), bounds_check=S - 1,
                                        oob_is_err=False).then_inc(ns["gathered"], 16)
                if b is not None:
                    pool.indirect_dma_start(out=xg[0:CAP2, 1, :], out_offset=None, in_=h_rows,
                                            in_offset=bass.IndirectOffsetOnAxis(idx_now[0:CAP2, 1:2], 0), bounds_check=S - 1,
                                            oob_is_err=False).then_inc(ns["gathered"], 16)

            pool.sem_inc(moe["rows_free"], PRIMED)
            pool.sem_inc(over["idle"], PRIMED)
            pool.wait_ge(route["tokens_made"], 1)
            gather(token_a[:, 1:2], token_b[:, 1:2], moe, 0)
            with pool.Fori(0, E) as e:
                pool.wait_ge(moe["x_turned"], e * 4 + 4)
                gather(token_a[:, bass.ds(e + 2, 1)], token_b[:, bass.ds(e + 2, 1)], moe, e + 1)
                store(choice_a[:, bass.ds(e, 1)], choice_b[:, bass.ds(e, 1)], moe, e)
                pool.wait_ge(moe["stored"], e * 32 + 32)
                pool.sem_inc(moe["rows_free"], 1)
            store(choice_a[:, E:E + 1], choice_b[:, E:E + 1], moe, E)
            pool.wait_ge(moe["x_turned"], 4 * (E + 1))
            pool.wait_ge(moe["stored"], 32 * (E + 1))
            most = pool.value_load(cnt[0:1, E:E + 1], min_val=0, max_val=S)
            with pool.If(most > CAP):
                with pool.Fori(0, E) as e:
                    for j in range(N_OVER):
                        gather(token_o[:, j, bass.ds(e + 1, 1)], None, over, e * N_OVER + j)
                        store(choice_o[:, j, bass.ds(e + 1, 1)], None, over, e * N_OVER + j)
                        pool.wait_ge(over["stored"], (e * N_OVER + j) * 16 + 16)
                        pool.sem_inc(over["idle"], 1)
            with pool.Else():
                pool.nop()
            pool.wait_ge(final["g_in"], 16)
            for t in range(NT):
                inverse_rms(final, t)
                if by_pool(t):
                    pool.wait_ge(final["scaled_act"], t + 1)
                    pool.tensor_tensor(facc[:, t, :], facc[:, t, :], gfin, ALU.mult).then_inc(final["gained"], 1)
                    pool.wait_ge(final["gained"], t + 1)

        @block.tensor
        def _(pe):
            def norm_turn(ns, buf, t, b):
                pe.wait_ge(ns["scaled"], t + 1)
                for k in range(KD):
                    last = pe.transpose(bank(b, 2)[:, k * P:(k + 1) * P], buf[:, t % 3, k * P:(k + 1) * P], ident[:, :])
                last.then_inc(ns["turned"], 1)

            pe.wait_ge(setup["ident_made"], 1)
            pe.wait_ge(setup["vec_in"], 7 * 16)
            pe.transpose(bank(4)[:, 0:P], vrows, ident[:, :])
            for a in range(4):
                pe.transpose(bank(5)[:, a * P:(a + 1) * P], brows[:, a, :], ident[:, :])
            for a in range(2):
                last = pe.transpose(bank(6)[:, a * P:(a + 1) * P], brows[:, 4 + a, :], ident[:, :])
            last.then_inc(setup["vecT_made"], 1)
            def mem_keys(c2):
                for k in range(KD):
                    last = pe.matmul(bank(4 + c2)[:, 0:MEM], wmkv[:, k, c2 * P:(c2 + 1) * P], memT[:, k, :],
                                     start=(k == 0), stop=(k == KD - 1))
                last.then_inc(setup["mkv_made"], 1)

            def mem_values(a):
                for k in range(KD):
                    last = pe.matmul(bank(6)[:, a * MEM:(a + 1) * MEM], memT[:, k, a * P:(a + 1) * P],
                                     wmkv[:, k, MEM:2 * MEM], start=(k == 0), stop=(k == KD - 1))
                if a == 1:
                    last.then_inc(setup["mkv_made"], 1)

            for t in range(NT + 2):
                if t >= 2:
                    pe.wait_ge(norms[0]["copied"], t - 1)
                norm_turn(norms[0], xn, t, 2 * (t % 2))
                if t == 5:
                    pe.wait_ge(setup["wmkv_in"], 16)
                    pe.wait_ge(setup["vecT_copied"], 3)
                if 5 <= t < 9:
                    (mem_keys if t < 7 else mem_values)((t - 5) % 2)
            pe.wait_ge(norms[0]["copied"], NT + 2)
            pe.wait_ge(setup["mkv_copied"], 5)

            def project(i, ns):
                pe.wait_ge(ns["w_in"], i * 48 + 48)
                for j in (1, 0):
                    for n in range(2):
                        for k in range(KD):
                            last = pe.matmul(bank(2 * j + n), wqkv[:, j, k, :], hT[:, k, n * HALF:(n + 1) * HALF],
                                             start=(k == 0), stop=(k == KD - 1))
                        last.then_inc(ns["proj"], 1)
                for n in range(2):
                    for t in range(4):
                        for k in range(KD):
                            last = pe.matmul(bank(4 + n)[:, t * P:(t + 1) * P], hT[:, k, (4 * n + t) * P:(4 * n + t + 1) * P],
                                             wqkv[:, 2, k, :], start=(k == 0), stop=(k == KD - 1))
                    last.then_inc(ns["proj"], 1)
                pe.wait_ge(ns["split"], i * SPLITS + SPLITS)

            def score(out, c2, t, first, w):
                pe.matmul(out, q_parts[:, c2, t * P:(t + 1) * P], k_high[:, c2, first:first + w],
                          start=True, stop=False)
                return pe.matmul(out, q_parts[:, c2, t * P:(t + 1) * P], k_low[:, c2, first:first + w],
                                 start=False, stop=True)

            with pe.Fori(0, DIFF_HEADS) as i:
                project(i, diff)

                def scores(t):
                    for c2 in range(2):
                        if t >= 1:
                            pe.wait_ge(diff["biased"], i * 16 + 2 * (t - 1) + c2 + 1)
                        for n in range(2):
                            last = score(bank(2 * c2 + n), c2, t, n * HALF, HALF)
                        last.then_inc(diff["scores"], 1)

                def turn(t):
                    if t == 0:
                        pe.wait_ge(diff["proj_copied"], i * COPIES + COPIES)
                    pe.wait_ge(diff["comb"], i * 8 + t + 1)
                    if t >= 1:
                        pe.wait_ge(diff["turned_copied"], i * 8 + t)
                    for a in range(NT):
                        last = pe.transpose(bank(4, 2)[:, a * P:(a + 1) * P], acomb[:, a * P:(a + 1) * P], ident[:, :])
                    last.then_inc(diff["turned"], 1)

                def weigh(t):
                    pe.wait_ge(diff["turned_copied"], i * 8 + t + 1)
                    if t >= 2:
                        pe.wait_ge(diff["out_copied"], i * 8 + t - 1)
                        pe.wait_ge(diff["squared"], i * 8 + t - 1)
                    for a in range(NT):
                        last = pe.matmul(bank(6 + t % 2)[:, 0:P], pT2[:, t % 2, a * P:(a + 1) * P], v_sb[:, a, :],
                                         start=(a == 0), stop=(a == NT - 1))
                    last.then_inc(diff["out"], 1)

                scores(0)
                for t in range(NT):
                    if t + 1 < NT:
                        scores(t + 1)
                    if t >= 1:
                        turn(t - 1)
                    if t >= 2:
                        weigh(t - 2)
                turn(NT - 1)
                weigh(NT - 2)
                weigh(NT - 1)
                pe.wait_ge(diff["out_copied"], i * 8 + 8)
                pe.wait_ge(diff["squared"], i * 8 + 8)

            with pe.Fori(0, NA_PAIRS) as i:
                project(i, na)

                def scores(u):
                    t, c2 = divmod(u, 2)
                    first, width, _ = na_window(t)
                    b = 2 * (u % 2)
                    if u >= 2:
                        pe.wait_ge(na["biased"], i * 16 + u - 1)
                    at, w = na_place(width)
                    for a in range(0, width, w):
                        last = score(bank(b, 2)[:, at + a:at + a + w], c2, t, first + a, w)
                    last.then_inc(na["scores"], 1)

                def turn(u):
                    chunks = -(-na_window(u // 2)[1] // P)
                    if u == 0:
                        pe.wait_ge(na["proj_copied"], i * COPIES + COPIES)
                    pe.wait_ge(na["exp"], i * 16 + u + 1)
                    if u >= 1:
                        pe.wait_ge(na["turned_copied"], i * 16 + u)
                    for a in range(chunks):
                        last = pe.transpose(bank(4, 2)[:, a * P:(a + 1) * P], sp[:, u % 4, a * P:(a + 1) * P], ident[:, :])
                    last.then_inc(na["turned"], 1)

                def weigh(u):
                    t, c2 = divmod(u, 2)
                    first, width, _ = na_window(t)
                    chunks = -(-width // P)
                    pe.wait_ge(na["turned_copied"], i * 16 + u + 1)
                    if u >= 2:
                        pe.wait_ge(na["out_copied"], i * 16 + u - 1)
                    for a in range(chunks):
                        last = pe.matmul(bank(6 + u % 2)[:, 0:HD], pT2[:, u % 2, a * P:(a + 1) * P],
                                         v_sb[:, first // P + a, c2 * HD:(c2 + 1) * HD], start=(a == 0), stop=(a == chunks - 1))
                    last.then_inc(na["out"], 1)

                scores(0)
                scores(1)
                for u in range(16):
                    turn(u)
                    if u + 2 < 16:
                        scores(u + 2)
                    if u >= 1:
                        weigh(u - 1)
                weigh(15)
                pe.wait_ge(na["out_copied"], i * 16 + 16)

            def mix_turn(t):
                pe.wait_ge(mixed["scaled"], t + 1)
                if t >= 1:
                    pe.wait_ge(mixed["copied"], t)
                for k in range(KD):
                    last = pe.transpose(bank(0, 2)[:, k * P:(k + 1) * P], mix[:, t, k * P:(k + 1) * P], ident[:, :])
                last.then_inc(mixed["turned"], 1)

            def norm1_turn(t):
                if t >= 1:
                    pe.wait_ge(norms[1]["copied"], t)
                norm_turn(norms[1], xn2, t, 2)

            mix_turn(0)
            pe.wait_ge(mixed["wout_in"], 64)
            for t in range(NT):
                if t + 1 < NT:
                    mix_turn(t + 1)
                pe.wait_ge(mixed["copied"], t + 1)
                if t >= 2:
                    pe.wait_ge(mixed["added"], t - 1)
                for n in range(2):
                    for k in range(KD):
                        last = pe.matmul(bank(4 + 2 * (t % 2) + n), hT[:, k, t * P:(t + 1) * P],
                                         wout[k][:, n * HALF:(n + 1) * HALF], start=(k == 0), stop=(k == KD - 1))
                last.then_inc(mixed["made"], 1)
                if t >= 1:
                    norm1_turn(t - 1)

            pe.wait_ge(cross["wmq_in"], 16)
            for n in range(2):
                if n == 1:
                    norm1_turn(NT - 1)
                    pe.wait_ge(mixed["added"], NT - 1)
                pe.wait_ge(norms[1]["copied"], 4 * n + 4)
                for c2 in range(2):
                    for k in range(KD):
                        last = pe.matmul(bank(4 * n + c2), wmq[:, k, c2 * P:(c2 + 1) * P], hT[:, k, n * HALF:(n + 1) * HALF],
                                         start=(k == 0), stop=(k == KD - 1))
                    last.then_inc(cross["q"], 1)
            pe.wait_ge(cross["q_copied"], 4)
            pe.wait_ge(cross["wmo_in"], 16)
            pe.wait_ge(route["w_in"], 16)

            def cross_scores(t):
                if t >= 1:
                    pe.wait_ge(cross["exp"], t)
                for hd in range(MH):
                    last = pe.matmul(bank(0, 2)[:, hd * MEM:(hd + 1) * MEM], qmT[:, hd // 2, t * P:(t + 1) * P],
                                     kmz[:, hd % 2, hd // 2, :], start=True, stop=True)
                last.then_inc(cross["scores"], 1)

            def cross_turn(t):
                pe.wait_ge(cross["exp"], t + 1)
                if t >= 3:
                    pe.wait_ge(norms[2]["copied"], t - 2)
                for a in range(8):
                    last = pe.transpose(bank(2, 2)[:, a * P:(a + 1) * P], mp[:, t % 2, a * P:(a + 1) * P], ident[:, :])
                last.then_inc(cross["turned"], 1)

            def cross_out(t):
                pe.wait_ge(cross["turned_copied"], t + 1)
                if t >= 1:
                    pe.wait_ge(cross["out_turned_copied"], t)
                for hd in range(MH):
                    for a in range(2):
                        last = pe.matmul(bank(4)[:, hd * HD:(hd + 1) * HD], mpT[:, (2 * hd + a) * P:(2 * hd + a + 1) * P],
                                         vmem[:, a, hd * HD:(hd + 1) * HD], start=(a == 0), stop=(a == 1))
                last.then_inc(cross["out"], 1)

            def cross_out_turn(t):
                pe.wait_ge(cross["out_copied"], t + 1)
                for a in range(2):
                    last = pe.transpose(bank(4)[:, MEM + a * P:MEM + (a + 1) * P], om[:, a * P:(a + 1) * P], ident[:, :])
                last.then_inc(cross["out_turned"], 1)

            def cross_made(t):
                pe.wait_ge(cross["out_turned_copied"], t + 1)
                if t >= 1:
                    pe.wait_ge(cross["added"], t)
                for n in range(2):
                    for k in range(2):
                        last = pe.matmul(bank(5 + n), omT[:, k * P:(k + 1) * P], wmo[:, k, n * HALF:(n + 1) * HALF],
                                         start=(k == 0), stop=(k == 1))
                last.then_inc(cross["made"], 1)

            def norm2_turn(t):
                pe.wait_ge(cross["turned_copied"], min(t + 3, NT))
                if t >= NT - 2:
                    pe.wait_ge(norms[2]["copied"], t)
                norm_turn(norms[2], xn2, t, 2)

            def places(t):
                pe.wait_ge(route["masked"], t + 1)
                if t == 0:
                    pe.wait_ge(route["consts"], 2)
                if t >= 1:
                    pe.wait_ge(route["slots"], t)
                for t2 in range(t + 1):
                    last = pe.matmul(bank(7)[:, MEM:MEM + E], ones if t2 < t else before, msum[:, t2 * E:(t2 + 1) * E],
                                     start=(t2 == 0), stop=(t2 == t))
                last.then_inc(route["placed"], 1)

            def logits(t):
                pe.wait_ge(norms[2]["copied"], t + 1)
                for k in range(KD):
                    last = pe.matmul(bank(7)[:, 0:E], hT[:, k, t * P:(t + 1) * P], wrt[:, k, :],
                                     start=(k == 0), stop=(k == KD - 1))
                last.then_inc(route["logits"], 1)

            def routed(t):
                if t >= 1:
                    places(t - 1)
                logits(t)

            cross_scores(0)
            for t in range(NT):
                cross_turn(t)
                if t + 1 < NT:
                    cross_scores(t + 1)
                if t >= 1:
                    cross_made(t - 1)
                cross_out(t)
                if t >= 2:
                    norm2_turn(t - 2)
                cross_out_turn(t)
                if t >= 3:
                    routed(t - 3)
            cross_made(NT - 1)
            norm2_turn(NT - 2)
            routed(NT - 3)
            norm2_turn(NT - 1)
            routed(NT - 2)
            routed(NT - 1)
            places(NT - 1)
            pe.wait_ge(route["slots"], NT)
            for t in range(NT):
                last = pe.matmul(bank(7)[:, 0:E], ones, msum[:, t * E:(t + 1) * E], start=(t == 0), stop=(t == NT - 1))
            last.then_inc(route["counted"], 1)
            for b in range(4):
                for a in range(3):
                    pe.transpose(bank(b)[:, a * P:(a + 1) * P], ident[:, :], ident[:, :])
            pe.wait_ge(route["cnt_made"], 1)

            def x_turn(ns, n, q, with_b=True):
                if q == 0:
                    pe.wait_ge(ns["gathered"], n * (32 if with_b else 16) + (32 if with_b else 16))
                    pe.wait_ge(ns["x_copied"], n * 4 + PRIMED)
                if q >= 2:
                    pe.wait_ge(ns["x_copied"], n * 4 + q - 1 + PRIMED)
                b = bank(4 + q % 2)
                for kk in range(2):
                    k = 2 * q + kk
                    last = pe.transpose(b[:, kk * CAP:kk * CAP + P], xg[:, 0, k * P:(k + 1) * P], ident[:, :])
                    if with_b:
                        last = pe.transpose(b[:, kk * CAP + P:(kk + 1) * CAP], xg[0:CAP2, 1, k * P:(k + 1) * P],
                                            ident[0:CAP2, 0:CAP2])
                last.then_inc(ns["x_turned"], 1)

            def y_turn(ns, n, q, copied, steps=4):
                half, a = divmod(q, 2) if steps == 4 else (q, 0)
                if a == 0:
                    pe.wait_ge(ns["y_copied"], copied - 4 + 4 * half + PRIMED)
                if q == 0:
                    pe.wait_ge(ns["y_moved"], n * steps + PRIMED)
                if q >= 2:
                    pe.wait_ge(ns["y_moved"], n * steps + q - 1 + PRIMED)
                    carried(pe)
                rows = P if a == 0 else CAP2
                for kk in range(4):
                    k = 4 * half + kk
                    last = pe.transpose(bank(6 + q % 2)[0:rows, kk * P:(kk + 1) * P], yT[:, k, a * P:a * P + rows], ident[:, :])
                last.then_inc(ns["y_turned"], 1)

            def up(ns, n, cols, between=None):
                for m in range(KF):
                    buf = wA if m < 4 else wB
                    if m == 0:
                        pe.wait_ge(ns["wA_in"], n * 32 + 32)
                    if m == 4:
                        pe.wait_ge(ns["wB_in"], n * 32 + 32)
                    if m >= 2:
                        pe.wait_ge(ns["gated"], n * 8 + m - 1)
                    for g in range(2):
                        for k in range(KD):
                            last = pe.matmul(bank(m % 2)[:, g * CAP:g * CAP + cols], buf[:, k, g, (m % 4) * P:(m % 4 + 1) * P],
                                             xT[:, k, 0:cols], start=(k == 0), stop=(k == KD - 1))
                    last.then_inc(ns["up"], 1)
                    if between:
                        between(m)

            def down(ns, n, cols, between=None):
                def part(m, k):
                    return pe.matmul(bank(2 + m % 2)[:, 0:cols], wD[:, k, m * P:(m + 1) * P], actT[:, k, 0:cols],
                                     start=(k == 0), stop=(k == KF - 1))

                pe.wait_ge(ns["wD_in"], n * 16 + 16)
                for m in range(2):
                    for k in range(KF - 1):
                        if m == 0:
                            pe.wait_ge(ns["act"], n * 8 + k + 1)
                        part(m, k)
                pe.wait_ge(ns["act"], n * 8 + KF)
                for m in range(2):
                    part(m, KF - 1).then_inc(ns["down"], 1)
                if between:
                    between(1)
                for m in range(2, KD):
                    pe.wait_ge(ns["y_copied"], n * 8 + m - 1 + PRIMED)
                    for k in range(KF):
                        last = part(m, k)
                    last.then_inc(ns["down"], 1)
                    if between:
                        between(m)

            def by_count(n, step, some=VARIANTS):
                if len(some) == 1:
                    step(some[0])
                    return
                half = len(some) // 2
                with pe.If(n <= some[half - 1]):
                    by_count(n, step, some[:half])
                    pe.nop()
                with pe.Else():
                    by_count(n, step, some[half:])
                    pe.nop()

            pe.wait_ge(final["cleared"], 2)
            for q in range(4):
                x_turn(moe, 0, q)
            with pe.Fori(0, E) as e:
                n = pe.value_load(cnt[0:1, bass.ds(e, 1)], min_val=0, max_val=S)
                y_turn(moe, e, 0, e * 8)
                y_turn(moe, e, 1, e * 8)
                pe.wait_ge(moe["x_copied"], e * 4 + 4 + PRIMED)

                def last_rows(m):
                    if 2 <= m <= 3:
                        y_turn(moe, e, m, e * 8)

                def next_rows(m):
                    if 1 <= m <= 4:
                        x_turn(moe, e + 1, m - 1)

                by_count(n, lambda cols: (up(moe, e, cols, last_rows), down(moe, e, cols, next_rows)))
            for q in range(4):
                y_turn(moe, E, q, E * 8)
            most = pe.value_load(cnt[0:1, E:E + 1], min_val=0, max_val=S)
            with pe.If(most > CAP):
                pe.wait_ge(moe["x_copied"], 4 * (E + 1) + PRIMED)
                pe.wait_ge(moe["y_moved"], 4 * (E + 1) + PRIMED)
                with pe.Fori(0, E) as e:
                    n = pe.value_load(cnt[0:1, bass.ds(e, 1)], min_val=0, max_val=S)
                    for j in range(N_OVER):
                        item = e * N_OVER + j
                        with pe.If(n > CAP + j * OVER):
                            for q in range(4):
                                x_turn(over, item, q, with_b=False)
                            pe.wait_ge(over["x_copied"], item * 4 + 4 + PRIMED)
                            up(over, item, OVER)
                            down(over, item, OVER)
                            for q in range(2):
                                y_turn(over, item, q, item * 8 + 8, steps=2)
                            pe.wait_ge(over["y_moved"], item * 2 + 2 + PRIMED)
                            carried(pe)
                        with pe.Else():
                            for s, v in ((over["x_turned"], 4), (over["up"], 8), (over["down"], 8), (over["y_turned"], 2)):
                                pe.sem_inc(s, v)
                        pe.nop()
            with pe.Else():
                pe.nop()

        @block.scalar
        def _(act):
            def square(ns, t, src, buf):
                if t >= 3:
                    act.wait_ge(ns["turned"], t - 2)
                    if ns is norms[2]:
                        act.wait_ge(h_stored[t % 3], 16 * (t // 3))
                act.activation(buf[:, t % 3, :], src, ACT.Square, scale=1.0 / math.sqrt(D), accum_out=ssq[:, t:t + 1]).then_inc(ns["squared"], 1)

            def scale(ns, t, src, buf):
                act.wait_ge(ns["rinv"], t + 1)
                act.activation(buf[:, t % 3, :], src, ACT.Copy, scale=rstd[:, t:t + 1]).then_inc(ns["scaled"], 1)

            def source0(t):
                return mrows[:, t, :] if t < 2 else xres[:, t - 2, :]

            def square0(t):
                if t >= 2:
                    act.wait_ge(tile_in[t - 2], 16)
                elif t == 0:
                    act.wait_ge(setup["mem_in"], 16)
                square(norms[0], t, source0(t), xn)

            square0(0)
            for t in range(NT + 2):
                if t + 1 < NT + 2:
                    square0(t + 1)
                scale(norms[0], t, source0(t), xn)
            act.wait_ge(setup["kz_zero"], 1)
            act.wait_ge(setup["mkv_made"], 3)
            for c2 in range(2):
                for h in range(2):
                    rows = slice(h * HD, (h + 1) * HD)
                    act.activation(kmz[rows, h, c2, :], bank(4 + c2)[rows, 0:MEM], ACT.Copy).then_inc(setup["mkv_copied"], 1)
            act.activation(vmem[:, :, :].rearrange("p a n -> p (a n)"), bank(6), ACT.Copy).then_inc(setup["mkv_copied"], 1)
            act.wait_ge(setup["lam_dots"], 2)
            act.activation(lam[:, 2:4], lam[:, 0:2], ACT.Exp).then_inc(setup["lam_exp"], 1)

            def project_copy(i, ns):
                def copied(ins):
                    ins.then_inc(ns["proj_copied"], 1)

                for n in range(2):
                    cols = slice(n * HALF, (n + 1) * HALF)
                    act.wait_ge(ns["proj"], i * 6 + 1 + n)
                    for h in range(2):
                        for half in range(2):
                            copied(act.activation(k_high[half * HD:(half + 1) * HD, h, cols],
                                                  bank(2 + n)[h * HD:(h + 1) * HD, :], ACT.Copy))
                for n in range(2):
                    cols = slice(n * HALF, (n + 1) * HALF)
                    act.wait_ge(ns["proj"], i * 6 + 3 + n)
                    for h in range(2):
                        copied(act.activation(q_parts[h * HD:(h + 1) * HD, h, cols],
                                              bank(n)[h * HD:(h + 1) * HD, :], ACT.Copy, scale=QSCALE))
                for n in range(2):
                    act.wait_ge(ns["proj"], i * 6 + 5 + n)
                    copied(act.activation(v_sb[:, 4 * n:4 * n + 4, :].rearrange("p t n -> p (t n)"), bank(4 + n), ACT.Copy))

            with act.Fori(0, DIFF_HEADS) as i:
                project_copy(i, diff)

                def copy_turned(t):
                    act.wait_ge(diff["turned"], i * 8 + t + 1)
                    if t >= 2:
                        act.wait_ge(diff["out"], i * 8 + t - 1)
                    act.activation(pT2[:, t % 2, :], bank(4, 2), ACT.Copy).then_inc(diff["turned_copied"], 1)

                def normalise(t):
                    act.wait_ge(diff["out"], i * 8 + t + 1)
                    act.activation(mix[:, t, bass.ds(i * P, P)], bank(6 + t % 2)[:, 0:P], ACT.Copy,
                                   scale=rinv8[:, 2 * (t % 4):2 * (t % 4) + 1]).then_inc(diff["out_copied"], 1)
                    if t >= 1:
                        act.wait_ge(diff["squared"], i * 8 + t)
                    act.activation(junk, bank(6 + t % 2)[:, 0:P], ACT.Square, scale=rinv8[:, 2 * (t % 4):2 * (t % 4) + 1],
                                   accum_out=ssq8[:, t:t + 1]).then_inc(diff["squared"], 1)

                for t in range(NT):
                    for c2 in range(2):
                        a = 2 * (t % 2) + c2
                        act.wait_ge(diff["biased"], i * 16 + 2 * t + c2 + 1)
                        act.activation(sp[:, a, :], sp[:, a, :], ACT.Exp, bias=nmax[:, a:a + 1],
                                       accum_out=rsum[:, a:a + 1]).then_inc(diff["exp"], 1)
                    if t >= 1:
                        copy_turned(t - 1)
                    if t >= 3:
                        normalise(t - 3)
                copy_turned(NT - 1)
                for t in range(NT - 3, NT):
                    normalise(t)
                act.wait_ge(diff["squared"], i * 8 + 8)
                carried(act)

            with act.Fori(0, NA_PAIRS) as i:
                project_copy(i, na)

                def copy_turned(u):
                    if u >= 2:
                        act.wait_ge(na["out"], i * 16 + u - 1)
                    act.wait_ge(na["turned"], i * 16 + u + 1)
                    w = -(-na_window(u // 2)[1] // P) * P
                    act.activation(pT2[:, u % 2, 0:w], bank(4, 2)[:, 0:w], ACT.Copy).then_inc(na["turned_copied"], 1)

                for u in range(16):
                    width = na_window(u // 2)[1]
                    act.wait_ge(na["biased"], i * 16 + u + 1)
                    act.activation(sp[:, u % 4, 0:width], sp[:, u % 4, 0:width], ACT.Exp, bias=nmax[:, u % 4:u % 4 + 1],
                                   accum_out=rsum[:, u % 4:u % 4 + 1]).then_inc(na["exp"], 1)
                    if u >= 1:
                        copy_turned(u - 1)
                copy_turned(15)

            for t in range(NT):
                act.wait_ge(mixed["added"], t + 1)
                square(norms[1], t, xres[:, t, :], xn2)
                scale(norms[1], t, xres[:, t, :], xn2)

            for n in range(2):
                for c2 in range(2):
                    act.wait_ge(cross["q"], 2 * n + c2 + 1)
                    act.activation(qmT[:, c2, n * HALF:(n + 1) * HALF], bank(4 * n + c2), ACT.Copy,
                                   scale=QSCALE).then_inc(cross["q_copied"], 1)

            def cross_exp(t):
                act.wait_ge(cross["max"], t + 1)
                if t >= 2:
                    act.wait_ge(cross["turned"], t - 1)
                for hd in range(MH):
                    last = act.activation(mp[:, t % 2, hd * MEM:(hd + 1) * MEM], bank(0, 2)[:, hd * MEM:(hd + 1) * MEM],
                                          ACT.Exp, bias=nmax[:, hd:hd + 1],
                                          accum_out=rsum8[:, 4 * (t % 2) + hd:4 * (t % 2) + hd + 1])
                last.then_inc(cross["exp"], 1)

            def square2(t):
                act.wait_ge(cross["added"], t + 1)
                square(norms[2], t, xres[:, t, :], xn2)

            cross_exp(0)
            for t in range(NT):
                act.wait_ge(cross["turned"], t + 1)
                act.activation(mpT, bank(2, 2), ACT.Copy).then_inc(cross["turned_copied"], 1)
                if t + 1 < NT:
                    cross_exp(t + 1)
                if t >= 1:
                    square2(t - 1)
                act.wait_ge(cross["out_turned"], t + 1)
                act.activation(omT, bank(4)[:, MEM:2 * MEM], ACT.Copy).then_inc(cross["out_turned_copied"], 1)
                if t >= 1:
                    scale(norms[2], t - 1, xres[:, t - 1, :], xn2)
            square2(NT - 1)
            scale(norms[2], NT - 1, xres[:, NT - 1, :], xn2)
            act.wait_ge(route["gate_in"], 1)
            act.activation(gates[:, :, :], gates[:, :, :], ACT.Exp).then_inc(route["gate_exp"], 1)

            def sigmoids(ns, n, between=None):
                for m in range(KF):
                    act.wait_ge(ns["gated"], n * 8 + m + 1)
                    if m >= 2:
                        act.wait_ge(ns["act"], n * 8 + m - 1)
                    act.activation(ep[:, m % 2, 2, :], ep[:, m % 2, 0, :], ACT.Sigmoid, scale=ALPHA).then_inc(ns["sig"], 1)
                    if between:
                        between(m)

            def y_move(ns, n, q, steps=4):
                if q == 0 and ns is moe:
                    act.wait_ge(ns["rows_free"], n + PRIMED)
                half, a = divmod(q, 2) if steps == 4 else (q, 0)
                rows = P if a == 0 else CAP2
                act.wait_ge(ns["y_turned"], n * steps + q + 1)
                act.activation(ysb[0:rows, a, half * HALF:(half + 1) * HALF], bank(6 + q % 2)[0:rows, :], ACT.Copy).then_inc(ns["y_moved"], 1)

            def bias_copy(ns, n, e):
                for m in range(KD):
                    act.wait_ge(ns["down"], n * 8 + m + 1)
                    act.activation(yT[:, m, :], bank(2 + m % 2)[:, 0:CAP], ACT.Identity,
                                   bias=b2T[:, bass.ds(e * 8 + m, 1)]).then_inc(ns["y_copied"], 1)

            for stage in (moe, over):
                act.sem_inc(stage["y_copied"], PRIMED)
                act.sem_inc(stage["y_moved"], PRIMED)
            act.wait_ge(final["cleared"], 2)
            with act.Fori(0, E) as e:
                sigmoids(moe, e, lambda m: y_move(moe, e, m) if m <= 3 else None)
                bias_copy(moe, e, e)
            for q in range(4):
                y_move(moe, E, q)
            most = act.value_load(cnt[0:1, E:E + 1], min_val=0, max_val=S)
            with act.If(most > CAP):
                with act.Fori(0, E) as e:
                    n = act.value_load(cnt[0:1, bass.ds(e, 1)], min_val=0, max_val=S)
                    for j in range(N_OVER):
                        item = e * N_OVER + j
                        with act.If(n > CAP + j * OVER):
                            sigmoids(over, item)
                            bias_copy(over, item, e)
                            for q in range(2):
                                y_move(over, item, q, steps=2)
                            act.wait_ge(over["y_moved"], item * 2 + 2 + PRIMED)
                            carried(act)
                        with act.Else():
                            for s, v in ((over["sig"], 8), (over["y_copied"], 8), (over["y_moved"], 2)):
                                act.sem_inc(s, v)
                        act.nop()
            with act.Else():
                act.nop()
            for t in range(NT):
                act.wait_ge(final["sum"], t + 1)
                act.activation(facc[:, t, :], xres[:, t, :], ACT.Square, scale=1.0 / math.sqrt(D),
                               accum_out=ssq[:, t:t + 1]).then_inc(final["squared"], 1)
                if by_pool(t):
                    act.wait_ge(final["rinv"], t + 1)
                    act.activation(facc[:, t, :], xres[:, t, :], ACT.Copy, scale=rstd[:, t:t + 1]).then_inc(final["scaled_act"], 1)

        def vector_program(dve):
            link = Link(dve, dve_link)

            def norm_copy(ns, t, b, dest, gain):
                dve.wait_ge(ns["turned"], t + 1)
                dve.tensor_tensor(dest, bank(b, 2).rearrange("p (k n) -> p k n", k=KD),
                                  gain.rearrange("p (k o) -> p k o", o=1).to_broadcast([P, KD, P]), ALU.mult).then_inc(ns["copied"], 1)

            def hT_tile(t):
                return hT[:, :, t * P:(t + 1) * P]

            dve.wait_ge(setup["vecT_made"], 1)
            dve.tensor_copy(vecT[:, :], bank(4)[:, 0:P]).then_inc(setup["vecT_copied"], 1)
            dve.tensor_copy(b1T[:, :], bank(5)).then_inc(setup["vecT_copied"], 1)
            dve.tensor_copy(b2T[:, :], bank(6)[:, 0:2 * P]).then_inc(setup["vecT_copied"], 1)
            dve.wait_ge(setup["vecT_copied"], 3)
            b1e = b1T[:, :].rearrange("p (e g m) -> p e g m", e=E, g=2)
            link(dve.tensor_scalar(b1e[:, :, 1, :], b1e[:, :, 1, :], 1.0, None, ALU.add))
            dve.memset(mixg[:, :], 1.0)
            link(dve.memset(lam[:, 4:6], 0.0))
            link(dve.tensor_scalar(mixg[:, 0:DIFF_HEADS], vecT[:, G_SUB:G_SUB + 1].to_broadcast([P, DIFF_HEADS]),
                                   1.0 - LAM_INIT, None, ALU.mult))
            dve.wait_ge(setup["lam_in"], 64)
            for a in range(2):
                dve.tensor_tensor_reduce(lamv[:, 2 * a, :], lamv[:, 2 * a, :], lamv[:, 2 * a + 1, :], 1.0, 0.0,
                                         ALU.mult, ALU.add, lam[:, a:a + 1]).then_inc(setup["lam_dots"], 1)

            def copy0(t):
                if t < 2:
                    norm_copy(norms[0], t, 2 * (t % 2), memT[:, :, t * P:(t + 1) * P], vecT[:, G_MEMKV:G_MEMKV + KD])
                else:
                    norm_copy(norms[0], t, 2 * (t % 2), hT_tile(t - 2), vecT[:, G_MIX:G_MIX + KD])

            for t in range(NT + 2):
                copy0(t)

            def split(i, ns):
                for n in range(2):
                    cols = slice(n * HALF, (n + 1) * HALF)
                    dve.wait_ge(ns["proj_copied"], i * COPIES + 4 * n + 4)
                    for h in range(2):
                        rows = slice(h * HD, (h + 1) * HD)
                        for half in range(2):
                            dve.tensor_tensor(k_low[half * HD:(half + 1) * HD, h, cols], bank(2 + n)[rows, :],
                                              k_high[rows, h, cols].bitcast(F32), ALU.subtract).then_inc(ns["split"], 1)
                for n in range(2):
                    cols = slice(n * HALF, (n + 1) * HALF)
                    dve.wait_ge(ns["proj_copied"], i * COPIES + 8 + 2 * n + 2)
                    for h in range(2):
                        rows, others = slice(h * HD, (h + 1) * HD), slice((1 - h) * HD, (2 - h) * HD)
                        dve.scalar_tensor_tensor(out=q_parts[others, h, cols], in0=bank(n)[rows, :], scalar=QSCALE,
                                                 in1=q_parts[rows, h, cols].bitcast(F32), op0=ALU.mult, op1=ALU.subtract).then_inc(ns["split"], 1)

            dve.wait_ge(setup["lam_exp"], 1)
            link(dve.tensor_tensor(lam[:, 4:5], lam[:, 3:4], lam[:, 2:3], ALU.subtract))
            link(dve.tensor_scalar(lam[:, 4:5], lam[:, 4:5], -LAM_INIT, None, ALU.add))
            neg_lam = lam[:, 4:5]

            dve.wait_ge(setup["alibi_made"], 1)
            dve.wait_ge(route["table_clear"], 16)
            link(dve.scalar_tensor_tensor(out=alibi, in0=alibi, scalar=-1.0, in1=alibi, op0=ALU.mult, op1=ALU.min))
            with dve.Fori(0, DIFF_HEADS) as i:
                link.enter(i, 1 + 16 + 16)
                link(dve.tensor_scalar(alibi, alibi, 0.25, None, ALU.mult))
                split(i, diff)

                def add_bias(t, c2):
                    a = 2 * (t % 2) + c2
                    if t >= 2:
                        dve.wait_ge(diff["comb"], i * 8 + t - 1)
                    dve.wait_ge(diff["scores"], i * 16 + 2 * t + c2 + 1)
                    carried(dve)
                    at = 896 - P * t
                    return link.mark(dve.tensor_tensor_reduce(sp[:, a, :], bank(2 * c2, 2), alibi[:, at:at + S], 1.0, LOWEST,
                                                                ALU.add, ALU.max, rmax[:, a:a + 1]))

                def negate_max(t, c2, biased):
                    a = 2 * (t % 2) + c2
                    link.need(biased)
                    dve.tensor_scalar(nmax[:, a:a + 1], rmax[:, a:a + 1], -1.0, None, ALU.mult).then_inc(diff["biased"], 1)

                def invert_sums(t):
                    a, b = 2 * (t % 2), 2 * (t % 4)
                    dve.wait_ge(diff["exp"], i * 16 + 2 * t + 2)
                    if t >= 4:
                        dve.wait_ge(diff["squared"], i * 8 + t - 3)
                    return link.mark(dve.reciprocal(rinv8[:, b:b + 2], rsum[:, a:a + 2]))

                def coefficient(t, inverted):
                    a, b = 2 * (t % 2), 2 * (t % 4)
                    link.need(inverted)
                    return link.mark(dve.tensor_scalar(coef[:, t % 2:t % 2 + 1], rsum[:, a:a + 1], rinv8[:, b + 1:b + 2],
                                                         neg_lam, ALU.mult, ALU.mult))

                def combine(t, ready):
                    a = 2 * (t % 2)
                    link.need(ready)
                    if t >= 1:
                        dve.wait_ge(diff["turned"], i * 8 + t)
                    dve.scalar_tensor_tensor(out=acomb, in0=sp[:, a + 1, :], scalar=coef[:, t % 2:t % 2 + 1], in1=sp[:, a, :],
                                             op0=ALU.mult, op1=ALU.add).then_inc(diff["comb"], 1)

                for t in range(NT):
                    biased = add_bias(t, 0)
                    if t >= 1:
                        inverted = invert_sums(t - 1)
                    negate_max(t, 0, biased)
                    biased = add_bias(t, 1)
                    if t >= 1:
                        ready = coefficient(t - 1, inverted)
                    negate_max(t, 1, biased)
                    if t >= 1:
                        combine(t - 1, ready)
                combine(NT - 1, coefficient(NT - 1, invert_sums(NT - 1)))
                dve.wait_ge(diff["squared"], i * 8 + 8)
                dve.tensor_scalar(sub_ms[:, bass.ds(i * NT, NT)], ssq8, 1.0 / P, None, ALU.mult).then_inc(diff["meansq"], 1)
                link.leave(DIFF_HEADS)

            dve.wait_ge(setup["small_in"], 32)
            dve.wait_ge(setup["pads_zero"], 1)
            rows_all = 2 * NA_TABLE // GRID_W
            with dve.Fori(0, NA_PAIRS) as i:
                link.enter(i, 1 + 4 + 16 + 16)
                dve.wait_ge(na["tab_in"], i * 16 + 16)
                tab_rows = tables.rearrange("p (r c) -> p r c", c=GRID_W)
                link(dve.tensor_tensor(tab_rows, tab_rows, cmask.rearrange("p (o c) -> p o c", o=1)
                                       .to_broadcast([P, rows_all, GRID_W]), ALU.add))
                for c2 in range(2):
                    link(dve.memset(na_tab[0:HD, c2, NA_EDGE + NA_ROWS * GRID_W:NA_TABLE], NEG))
                    link(dve.memset(na_tab[HD:P, c2, NA_EDGE:NA_EDGE + GRID_W], NEG))
                split(i, na)

                def add_bias(u):
                    t, c2 = divmod(u, 2)
                    _, width, at = na_window(t)
                    placed = na_place(width)[0]
                    if u >= 4:
                        dve.wait_ge(na["turned"], i * 16 + u - 3)
                    dve.wait_ge(na["scores"], i * 16 + u + 1)
                    carried(dve)
                    return link.mark(dve.tensor_tensor_reduce(sp[:, u % 4, 0:width], bank(2 * (u % 2), 2)[:, placed:placed + width],
                                                                na_tab[:, c2, at:at + width], 1.0, LOWEST, ALU.add, ALU.max,
                                                                rmax[:, u % 4:u % 4 + 1]))

                def negate_max(u, biased):
                    link.need(biased)
                    dve.tensor_scalar(nmax[:, u % 4:u % 4 + 1], rmax[:, u % 4:u % 4 + 1], -1.0, None, ALU.mult).then_inc(na["biased"], 1)

                def invert_sum(u):
                    dve.wait_ge(na["out"], i * 16 + u + 1)
                    return link.mark(dve.reciprocal(rinv[:, u % 4:u % 4 + 1], rsum[:, u % 4:u % 4 + 1]))

                def normalise(u, inverted):
                    t, c2 = divmod(u, 2)
                    link.need(inverted)
                    dve.tensor_scalar(mix[:, t, bass.ds(HALF + c2 * HD + i * P, HD)], bank(6 + u % 2)[:, 0:HD],
                                      rinv[:, u % 4:u % 4 + 1], None, ALU.mult).then_inc(na["out_copied"], 1)

                for u in range(16):
                    biased = add_bias(u)
                    if u >= 3:
                        inverted = invert_sum(u - 3)
                    negate_max(u, biased)
                    if u >= 3:
                        normalise(u - 3, inverted)
                for u in range(13, 16):
                    normalise(u, invert_sum(u))
                link.leave(NA_PAIRS)

            dve.wait_ge(mixed["sub_rinv"], 1)

            def mix_scale(t):
                v = mix[:, t, 0:DIFF_HEADS * P].rearrange("p (h v) -> p h v", h=DIFF_HEADS)
                dve.tensor_tensor(v, v, sub_rs.rearrange("p (h t o) -> p h t o", h=DIFF_HEADS, o=1)[:, :, t, :]
                                  .to_broadcast([P, DIFF_HEADS, P]), ALU.mult).then_inc(mixed["scaled"], 1)

            def mix_copy(t):
                dve.wait_ge(mixed["turned"], t + 1)
                dve.tensor_tensor(hT_tile(t), bank(0, 2).rearrange("p (k n) -> p k n", k=KD),
                                  mixg[:, :].rearrange("p (k o) -> p k o", o=1).to_broadcast([P, KD, P]),
                                  ALU.mult).then_inc(mixed["copied"], 1)

            def copy1(t):
                norm_copy(norms[1], t, 2, hT_tile(t), vecT[:, G_MEMQ:G_MEMQ + KD])

            mix_scale(0)
            mix_scale(1)
            mix_copy(0)
            for t in range(NT):
                if t + 2 < NT:
                    mix_scale(t + 2)
                if t + 1 < NT:
                    mix_copy(t + 1)
                dve.wait_ge(mixed["made"], t + 1)
                dve.tensor_tensor(xres[:, t, :], xres[:, t, :], bank(4 + 2 * (t % 2), 2), ALU.add).then_inc(mixed["added"], 1)
                if t >= 1:
                    copy1(t - 1)
            copy1(NT - 1)

            def cross_max_of(t):
                dve.wait_ge(cross["scores"], t + 1)
                link(dve.tensor_reduce(cross_max, bank(0, 2).rearrange("p (h n) -> p h n", h=MH), AX.X, ALU.max))
                if t >= 1:
                    dve.wait_ge(cross["exp"], t)
                dve.tensor_scalar(nmax, cross_max, -1.0, None, ALU.mult).then_inc(cross["max"], 1)

            def cross_add(t):
                dve.wait_ge(cross["made"], t + 1)
                dve.tensor_tensor(xres[:, t, :], xres[:, t, :], bank(5, 2), ALU.add).then_inc(cross["added"], 1)

            def copy2(t):
                norm_copy(norms[2], t, 2, hT_tile(t), vecT[:, G_FFN:G_FFN + KD])

            def pick(t):
                a = t % 2
                link(dve.tensor_tensor(logit[:, a, :], bank(7)[:, 0:E], brt[:, :], ALU.add))
                link(dve.max(top8[:, t, :], logit[:, a, :]))
                link(dve.max_index(top8i[:, t, :], top8[:, t, :], logit[:, a, :]))
                link(dve.tensor_copy(chosen[:, t, :], top8i[:, t, 0:TOPK]))
                link(dve.tensor_tensor(oneh[:, a, :, :], iota_e.rearrange("p (o e) -> p o e", o=1).to_broadcast([P, TOPK, E]),
                                       chosen[:, t, :].rearrange("p (k o) -> p k o", o=1).to_broadcast([P, TOPK, E]), ALU.is_equal))
                dve.tensor_reduce(msum[:, t * E:(t + 1) * E], oneh[:, a, :, :].rearrange("p k e -> p e k"),
                                  AX.X, ALU.add).then_inc(route["masked"], 1)

            def place(t):
                a = t % 2
                dve.wait_ge(route["placed"], t + 1)
                link(dve.scalar_tensor_tensor(out=slotm, in0=bank(7)[:, MEM:MEM + E], scalar=float(EC), in1=iota_e,
                                              op0=ALU.mult, op1=ALU.add))
                link(dve.tensor_tensor(prod, oneh[:, a, :, :], slotm.rearrange("p (o e) -> p o e", o=1)
                                       .to_broadcast([P, TOPK, E]), ALU.mult))
                link(dve.tensor_reduce(slot_f[:, t, :], prod, AX.X, ALU.add))
                dve.tensor_scalar(slot_u[:, t, :], slot_f[:, t, :], 1.0, None, ALU.add).then_inc(route["slots"], 1)

            def routed(t):
                dve.wait_ge(route["logits"], t + 1)
                if t >= 1:
                    place(t - 1)
                pick(t)

            cross_max_of(0)
            dve.wait_ge(route["consts"], 2)
            for t in range(NT):
                if t + 1 < NT:
                    cross_max_of(t + 1)
                if t >= 1:
                    cross_add(t - 1)
                dve.wait_ge(cross["exp"], t + 1)
                link(dve.reciprocal(rinv, rsum8[:, 4 * (t % 2):4 * (t % 2) + 4]))
                dve.wait_ge(cross["out"], t + 1)
                dve.tensor_tensor(om.rearrange("p (h d) -> p h d", h=MH), bank(4)[:, 0:MEM].rearrange("p (h d) -> p h d", h=MH),
                                  rinv.rearrange("p (h o) -> p h o", o=1).to_broadcast([P, MH, HD]), ALU.mult).then_inc(
                                      cross["out_copied"], 1)
                if t >= 2:
                    copy2(t - 2)
                if t >= 3:
                    routed(t - 3)
            cross_add(NT - 1)
            copy2(NT - 2)
            routed(NT - 3)
            copy2(NT - 1)
            routed(NT - 2)
            routed(NT - 1)
            dve.tensor_tensor(gates[:, :, :], top8[:, :, 0:TOPK], top8[:, :, 0:1].to_broadcast([P, NT, TOPK]),
                              ALU.subtract).then_inc(route["gate_in"], 1)
            place(NT - 1)
            dve.wait_ge(route["counted"], 1)
            link(dve.tensor_copy(cnt[:, 0:E], bank(7)[:, 0:E]))
            dve.tensor_reduce(cnt[:, E:E + 1], cnt[:, 0:E], AX.X, ALU.max).then_inc(route["cnt_made"], 1)
            dve.wait_ge(route["gate_exp"], 1)
            gsum = st[:, 58:58 + NT]
            link(dve.tensor_reduce(gsum, gates[:, :, :], AX.X, ALU.add))
            link(dve.reciprocal(gsum, gsum))
            dve.tensor_tensor(gates[:, :, :], gates[:, :, :], gsum.rearrange("p (t o) -> p t o", o=1)
                              .to_broadcast([P, NT, TOPK]), ALU.mult).then_inc(route["gates_made"], 1)

            dve.wait_ge(route["idx_in"], 48)
            link(dve.tensor_scalar(token_all, choice_all, int(math.log2(TOPK)), None, ALU.logical_shift_right))
            dve.sem_inc(route["tokens_made"], 1)

            def x_copy(ns, n, cols=CAP):
                for q in range(4):
                    dve.wait_ge(ns["x_turned"], n * 4 + q + 1)
                    dve.tensor_tensor(xT[:, 2 * q:2 * q + 2, 0:cols], bank(4 + q % 2)[:, 0:2 * CAP].rearrange("p (k n) -> p k n", k=2)[:, :, 0:cols],
                                      vecT[:, G_FFN + 2 * q:G_FFN + 2 * q + 2].rearrange("p (k o) -> p k o", o=1)
                                      .to_broadcast([P, 2, cols]), ALU.mult).then_inc(ns["x_copied"], 1)

            def gate_up(ns, n, e):
                def finish(m):
                    dve.wait_ge(ns["sig"], n * 8 + m + 1)
                    link(dve.tensor_tensor(ep[:, m % 2, 3, :], ep[:, m % 2, 0, :], ep[:, m % 2, 2, :], ALU.mult))
                    dve.scalar_tensor_tensor(out=actT[:, m, :], in0=ep[:, m % 2, 1, :], scalar=1.0 - LIMIT,
                                             in1=ep[:, m % 2, 3, :], op0=ALU.max, op1=ALU.mult).then_inc(ns["act"], 1)

                for m in range(KF):
                    if m >= 2:
                        dve.wait_ge(ns["act"], n * 8 + m - 1)
                    dve.wait_ge(ns["up"], n * 8 + m + 1)
                    dve.tensor_scalar(ep[:, m % 2, 1, :], bank(m % 2)[:, CAP:2 * CAP], b1T[:, bass.ds(e * 16 + 8 + m, 1)],
                                      1.0 + LIMIT, ALU.add, ALU.min)
                    dve.tensor_scalar(ep[:, m % 2, 0, :], bank(m % 2)[:, 0:CAP], b1T[:, bass.ds(e * 16 + m, 1)],
                                      LIMIT, ALU.add, ALU.min).then_inc(ns["gated"], 1)
                    if m >= 1:
                        finish(m - 1)
                finish(KF - 1)
                dve.wait_ge(ns["act"], n * 8 + 8)
                carried(dve)

            for stage in (moe, over):
                dve.sem_inc(stage["x_copied"], PRIMED)
            dve.wait_ge(final["cleared"], 2)
            x_copy(moe, 0)
            with dve.Fori(0, E) as e:
                link.enter(e, 8)
                gate_up(moe, e, e)
                x_copy(moe, e + 1)
                link.leave(E)
            most = dve.value_load(cnt[0:1, E:E + 1], min_val=0, max_val=S)
            over_base = link.base
            with dve.If(most > CAP):
                with dve.Fori(0, E) as e:
                    n = dve.value_load(cnt[0:1, bass.ds(e, 1)], min_val=0, max_val=S)
                    for j in range(N_OVER):
                        item = e * N_OVER + j
                        with dve.If(n > CAP + j * OVER):
                            link.base, link.n = over_base, 0
                            link.enter(item, 8)
                            x_copy(over, item, OVER)
                            gate_up(over, item, e)
                            dve.wait_ge(over["act"], item * 8 + 8)
                            carried(dve)
                            link.leave(0)
                        with dve.Else():
                            dve.sem_inc(dve_link, 8)
                            for s, v in ((over["x_copied"], 4), (over["gated"], 8), (over["act"], 8)):
                                dve.sem_inc(s, v)
                        dve.nop()
            with dve.Else():
                dve.sem_inc(dve_link, 8 * E * N_OVER)
            link.base, link.n = over_base + 8 * E * N_OVER, 0

            dve.wait_ge(final["g_in"], 16)
            dve.wait_ge(moe["y_copied"], 8 * E + PRIMED)

            for t in range(NT):
                dve.wait_ge(tile_in[t], 32)
                for k in range(TOPK):
                    ins = dve.scalar_tensor_tensor(out=xres[:, t, :], in0=yg[(t % 4) * TOPK + k], scalar=gates[:, t, k:k + 1],
                                                   in1=xres[:, t, :], op0=ALU.mult, op1=ALU.add)
                    if k < TOPK - 1:
                        link(ins)
                    else:
                        ins.then_inc(final["sum"], 1)
            for t in range(POOL_TILES, NT):
                dve.wait_ge(final["rinv"], t + 1)
                dve.scalar_tensor_tensor(out=facc[:, t, :], in0=xres[:, t, :], scalar=rstd[:, t:t + 1], in1=gfin,
                                         op0=ALU.mult, op1=ALU.mult).then_inc(final["scaled"], 1)

        block.vector(vector_program)


_INS = ["x", "mem", "norm_mix_g", "w_in", "lambda_q1", "lambda_k1", "lambda_q2", "lambda_k2", "subln_g", "rpb",
        "w_out", "norm_mem_q_g", "norm_mem_kv_g", "w_mq", "w_mkv", "w_mo", "norm_ffn_g", "w_router", "b_router",
        "w1", "b1", "w2", "b2", "norm_final_g"]


def column_mask():
    import numpy as np
    col = np.arange(2 * GRID_W) % GRID_W
    start = np.clip(col - NA_COLS // 2, 0, GRID_W - NA_COLS)
    key = np.arange(GRID_W)
    inside = (key[None] >= start[:, None]) & (key[None] < start[:, None] + NA_COLS)
    return np.where(inside, 0.0, NEG).astype(np.float32)


def kernel(**inputs):
    import numpy as np
    from concourse import bacc
    from concourse.bass_utils import run_bass_kernel_spmd

    nc = bacc.Bacc("TRN2", target_bir_lowering=False, num_devices=1)
    arrays, args = {}, []
    for name in _INS + ["col_mask"]:
        a = column_mask() if name == "col_mask" else np.ascontiguousarray(inputs[name])
        arrays[f"in_{name}"] = a
        args.append(nc.dram_tensor(f"in_{name}", a.shape, mybir.dt.from_np(a.dtype), kind="ExternalInput").ap())
    args.append(nc.dram_tensor("out_y", (1, S, D), F32, kind="ExternalOutput").ap())
    encoder_layer(nc, *args)
    r = run_bass_kernel_spmd(nc, [arrays], core_ids=[0])
    return r.results[0]["out_y"]
```
